# Optimizing a Trainium2 kernel written in Bass

```python
import math
import jax, jax.numpy as jnp
from jax import lax
import numpy as np

D_MODEL = 1024
BATCH = 1
SEQ = 1024
DEPTH = 2

N_META = 16
BLK = 128
PAD_LEAD = BLK - N_META
D_MIX = 2 * D_MODEL
N_MIXERS = 4
D_GROUP = D_MIX // N_MIXERS
HEAD_DIM = 64
N_HG = D_GROUP // HEAD_DIM

FOX_HEADS = N_HG
MLA_HEADS = N_HG
MLA_NOPE = HEAD_DIM
MLA_ROPE = 32
MLA_V = HEAD_DIM
MLA_Q_RANK = D_MODEL // 4
MLA_KV_RANK = D_MODEL // 8
DSA_HEADS = N_HG
DSA_KV = 2
IDX_HEADS = 8
IDX_DIM = 64
TOPK_MAX = 256
SWA_HEADS = N_HG
SWA_KV = 2
WINDOW = 128
REL_BUCKETS = 32
REL_MAX_DIST = 128
ROPE_BASE = 10000.0
LN_EPS = 1e-5
RMS_EPS = 1e-6
NEG = -1e30
ALPHA = (2 * DEPTH) ** 0.25
BETA = (8 * DEPTH) ** -0.25

IN_COLS = (
    ('a_q', FOX_HEADS * HEAD_DIM), ('a_k', FOX_HEADS * HEAD_DIM), ('a_v', FOX_HEADS * HEAD_DIM),
    ('a_f', FOX_HEADS), ('a_g', D_GROUP),
    ('b_cq', MLA_Q_RANK), ('b_ckv', MLA_KV_RANK), ('b_kr', MLA_ROPE), ('b_g', D_GROUP),
    ('c_q', DSA_HEADS * HEAD_DIM), ('c_k', DSA_KV * HEAD_DIM), ('c_v', DSA_KV * HEAD_DIM),
    ('c_iq', IDX_HEADS * IDX_DIM), ('c_ik', IDX_DIM), ('c_iw', IDX_HEADS), ('c_g', D_GROUP),
    ('d_q', SWA_HEADS * HEAD_DIM), ('d_k', SWA_KV * HEAD_DIM), ('d_v', SWA_KV * HEAD_DIM), ('d_g', D_GROUP),
)
VALUE_COLS = ('a_v', 'c_v', 'd_v')
D_IN = sum(s for _, s in IN_COLS)

kernel_name = 'hymba_fox_mla_dsa_swa_deepnorm'

def split_cols(h):
    out = {}
    off = 0
    for name, size in IN_COLS:
        out[name] = h[..., off:off + size]
        off += size
    return out

def layer_norm(x, g, b):
    xf = x.astype(jnp.float32)
    mu = jnp.mean(xf, axis=-1, keepdims=True)
    var = jnp.mean(jnp.square(xf - mu), axis=-1, keepdims=True)
    y = (xf - mu) * lax.rsqrt(var + LN_EPS) * g.astype(jnp.float32) + b.astype(jnp.float32)
    return y.astype(x.dtype)

def rms_norm(x, g):
    xf = x.astype(jnp.float32)
    y = xf * lax.rsqrt(jnp.mean(jnp.square(xf), axis=-1, keepdims=True) + RMS_EPS) * g.astype(jnp.float32)
    return y.astype(x.dtype)

def rope(x, pos):
    half = x.shape[-1] // 2
    freqs = ROPE_BASE ** (-jnp.arange(half, dtype=jnp.float32) / half)
    ang = pos.astype(jnp.float32)[:, None] * freqs[None, :]
    cos = jnp.cos(ang)[:, None, :]
    sin = jnp.sin(ang)[:, None, :]
    x1 = x[..., :half].astype(jnp.float32)
    x2 = x[..., half:].astype(jnp.float32)
    return jnp.concatenate([x1 * cos - x2 * sin, x1 * sin + x2 * cos], axis=-1).astype(x.dtype)

def t5_bucket(dist):
    n = jnp.maximum(dist, 0)
    max_exact = REL_BUCKETS // 2
    nf = jnp.maximum(n, 1).astype(jnp.float32)
    large = max_exact + (jnp.log(nf / max_exact) / math.log(REL_MAX_DIST / max_exact)
                         * (REL_BUCKETS - max_exact)).astype(jnp.int32)
    large = jnp.minimum(large, REL_BUCKETS - 1)
    return jnp.where(n < max_exact, n, large)

def causal_dense_attention(q, k, v, key_valid, scale, decay=None):
    B, P, H, _ = q.shape
    dv = v.shape[-1]
    nb = P // BLK
    kpos = jnp.arange(P)

    def one_block(i):
        start = i * BLK
        qb = lax.dynamic_slice_in_dim(q, start, BLK, axis=1)
        tpos = start + jnp.arange(BLK)
        logits = jnp.einsum('bqhd,bkhd->bhqk', qb, k, preferred_element_type=jnp.float32) * scale
        if decay is not None:
            cq = lax.dynamic_slice_in_dim(decay, start, BLK, axis=2)
            logits = logits + cq[..., None] - decay[:, :, None, :]
        mask = (kpos[None, :] <= tpos[:, None]) & key_valid[None, :]
        probs = jax.nn.softmax(jnp.where(mask, logits, NEG), axis=-1)
        return jnp.einsum('bhqk,bkhd->bqhd', probs.astype(v.dtype), v)

    out = lax.map(one_block, jnp.arange(nb))
    return jnp.transpose(out, (1, 0, 2, 3, 4)).reshape(B, P, H * dv)

def mla_attention(c_q, c_kv, k_rope, g_q, g_kv, w_uq, w_ukv, pos, key_valid):
    B, P, _ = c_q.shape
    q = (rms_norm(c_q, g_q) @ w_uq).reshape(B, P, MLA_HEADS, MLA_NOPE + MLA_ROPE)
    q = jnp.concatenate([q[..., :MLA_NOPE], rope(q[..., MLA_NOPE:], pos)], axis=-1)
    kv = (rms_norm(c_kv, g_kv) @ w_ukv).reshape(B, P, MLA_HEADS, MLA_NOPE + MLA_V)
    k_pe = jnp.broadcast_to(rope(k_rope[:, :, None, :], pos), (B, P, MLA_HEADS, MLA_ROPE))
    k = jnp.concatenate([kv[..., :MLA_NOPE], k_pe], axis=-1)
    v = kv[..., MLA_NOPE:]
    return causal_dense_attention(q, k, v, key_valid, (MLA_NOPE + MLA_ROPE) ** -0.5)

def dsa_sparse_attention(q, k, v, iq, ik, iw, key_valid, rel_bias_c, top_k):
    B, P, G, R, d = q.shape
    nb = P // BLK
    kpos = jnp.arange(P)
    gather = jax.vmap(lambda arr, idx: arr[idx])

    def one_block(i):
        start = i * BLK
        tpos = start + jnp.arange(BLK)
        qb = lax.dynamic_slice_in_dim(q, start, BLK, axis=1)
        iqb = lax.dynamic_slice_in_dim(iq, start, BLK, axis=1)
        iwb = lax.dynamic_slice_in_dim(iw, start, BLK, axis=1)
        s = jnp.einsum('bqhd,bkd->bqhk', iqb, ik, preferred_element_type=jnp.float32) * IDX_DIM ** -0.5
        score = jnp.einsum('bqhk,bqh->bqk', jax.nn.relu(s), iwb.astype(jnp.float32)) * IDX_HEADS ** -0.5
        adm = (kpos[None, :] <= tpos[:, None]) & key_valid[None, :]
        score = jnp.where(adm[None], score, NEG)
        _, idx = lax.top_k(score, top_k)
        k_sel = gather(k, idx)
        v_sel = gather(v, idx)
        logits = jnp.einsum('bqgrd,bqkgd->bgrqk', qb, k_sel, preferred_element_type=jnp.float32) * d ** -0.5
        bias = rel_bias_c[t5_bucket(tpos[None, :, None] - idx)].astype(jnp.float32)
        bias = bias.reshape(B, BLK, top_k, G, R).transpose(0, 3, 4, 1, 2)
        sel_ok = (idx <= tpos[None, :, None]) & key_valid[idx]
        logits = jnp.where(sel_ok[:, None, None], logits + bias, NEG)
        probs = jax.nn.softmax(logits, axis=-1)
        return jnp.einsum('bgrqk,bqkgd->bqgrd', probs.astype(v.dtype), v_sel)

    out = lax.map(one_block, jnp.arange(nb))
    return jnp.transpose(out, (1, 0, 2, 3, 4, 5)).reshape(B, P, G * R * d)

def sliding_window_sink_attention(q, k, v, key_valid, rel_bias_d, sinks):
    B, P, G, R, d = q.shape
    nb = P // BLK
    qb = q.reshape(B, nb, BLK, G, R, d)
    kb = k.reshape(B, nb, BLK, G, d)
    vb = v.reshape(B, nb, BLK, G, d)
    zero = jnp.zeros_like(kb[:, :1])
    kk = jnp.concatenate([jnp.concatenate([zero, kb[:, :-1]], axis=1), kb], axis=2)
    vv = jnp.concatenate([jnp.concatenate([zero, vb[:, :-1]], axis=1), vb], axis=2)
    qi = jnp.arange(BLK)
    kj = jnp.arange(2 * BLK)
    dist = BLK + qi[:, None] - kj[None, :]
    kabs = (jnp.arange(nb)[:, None] - 1) * BLK + kj[None, :]
    kval = (kabs >= 0) & key_valid[jnp.clip(kabs, 0, P - 1)]
    mask = ((dist >= 0) & (dist < WINDOW))[None] & kval[:, None, :]
    bias = rel_bias_d[t5_bucket(dist)].astype(jnp.float32)
    bias = bias.reshape(BLK, 2 * BLK, G, R).transpose(2, 3, 0, 1)
    logits = jnp.einsum('bnqgrd,bnkgd->bngrqk', qb, kk, preferred_element_type=jnp.float32) * d ** -0.5 + bias
    logits = jnp.where(mask[None, :, None, None], logits, NEG)
    sink = sinks.astype(jnp.float32).reshape(G, R)[None, None, :, :, None, None]
    m = jnp.maximum(jnp.max(logits, axis=-1, keepdims=True), sink)
    e = jnp.exp(logits - m)
    probs = e / (jnp.sum(e, axis=-1, keepdims=True) + jnp.exp(sink - m))
    out = jnp.einsum('bngrqk,bnkgd->bnqgrd', probs.astype(v.dtype), vv)
    return out.reshape(B, P, G * R * d)

def hybrid_layer(x, pos, key_valid, rel_bias, top_k, w_in, b_f, g_q, g_kv, w_uq, w_ukv, sinks, w_out, ln_g, ln_b):
    B, P, _ = x.shape
    h = split_cols(x @ w_in)
    qa = h['a_q'].reshape(B, P, FOX_HEADS, HEAD_DIM)
    ka = h['a_k'].reshape(B, P, FOX_HEADS, HEAD_DIM)
    va = h['a_v'].reshape(B, P, FOX_HEADS, HEAD_DIM)
    logf = jax.nn.log_sigmoid(h['a_f'].astype(jnp.float32) + b_f.astype(jnp.float32))
    decay = jnp.transpose(jnp.cumsum(logf, axis=1), (0, 2, 1))
    out_a = causal_dense_attention(qa, ka, va, key_valid, HEAD_DIM ** -0.5, decay)
    out_b = mla_attention(h['b_cq'], h['b_ckv'], h['b_kr'], g_q, g_kv, w_uq, w_ukv, pos, key_valid)
    rc = DSA_HEADS // DSA_KV
    out_c = dsa_sparse_attention(
        h['c_q'].reshape(B, P, DSA_KV, rc, HEAD_DIM),
        h['c_k'].reshape(B, P, DSA_KV, HEAD_DIM),
        h['c_v'].reshape(B, P, DSA_KV, HEAD_DIM),
        h['c_iq'].reshape(B, P, IDX_HEADS, IDX_DIM), h['c_ik'], h['c_iw'],
        key_valid, rel_bias[:, :DSA_HEADS], top_k)
    rd = SWA_HEADS // SWA_KV
    out_d = sliding_window_sink_attention(
        h['d_q'].reshape(B, P, SWA_KV, rd, HEAD_DIM),
        h['d_k'].reshape(B, P, SWA_KV, HEAD_DIM),
        h['d_v'].reshape(B, P, SWA_KV, HEAD_DIM),
        key_valid, rel_bias[:, DSA_HEADS:], sinks)
    mixed = jnp.concatenate([
        out_a * jax.nn.silu(h['a_g']), out_b * jax.nn.silu(h['b_g']),
        out_c * jax.nn.silu(h['c_g']), out_d * jax.nn.silu(h['d_g'])], axis=-1)
    y = mixed @ w_out
    return layer_norm(ALPHA * x + y, ln_g, ln_b)

def setup_inputs(seed: int = 0) -> dict:
    key = jax.random.key(seed)
    ks = jax.random.split(key, 16)
    f32 = jnp.float32
    col_scale = jnp.asarray(np.concatenate(
        [np.full((s,), BETA if name in VALUE_COLS else 1.0, dtype=np.float32) for name, s in IN_COLS]))
    ukv_scale = jnp.concatenate([jnp.ones((MLA_HEADS, MLA_NOPE), f32),
                                 jnp.full((MLA_HEADS, MLA_V), BETA, f32)], axis=-1).reshape(-1)
    return {
        'x': jax.random.normal(ks[0], (BATCH, SEQ, D_MODEL), f32),
        'meta_tokens': jax.random.normal(ks[1], (N_META, D_MODEL), f32),
        'ln0_g': 1.0 + 0.02 * jax.random.normal(ks[2], (D_MODEL,), f32),
        'ln0_b': 0.02 * jax.random.normal(ks[3], (D_MODEL,), f32),
        'rel_bias': 0.5 * jax.random.normal(ks[4], (REL_BUCKETS, DSA_HEADS + SWA_HEADS), f32),
        'w_in': jax.random.normal(ks[5], (DEPTH, D_MODEL, D_IN), f32) * D_MODEL ** -0.5 * col_scale,
        'b_f': 1.0 + 0.1 * jax.random.normal(ks[6], (DEPTH, FOX_HEADS), f32),
        'mla_gq': 1.0 + 0.02 * jax.random.normal(ks[7], (DEPTH, MLA_Q_RANK), f32),
        'mla_gkv': 1.0 + 0.02 * jax.random.normal(ks[8], (DEPTH, MLA_KV_RANK), f32),
        'w_uq': jax.random.normal(ks[9], (DEPTH, MLA_Q_RANK, MLA_HEADS * (MLA_NOPE + MLA_ROPE)), f32) * MLA_Q_RANK ** -0.5,
        'w_ukv': jax.random.normal(ks[10], (DEPTH, MLA_KV_RANK, MLA_HEADS * (MLA_NOPE + MLA_V)), f32) * MLA_KV_RANK ** -0.5 * ukv_scale,
        'sinks': 0.5 * jax.random.normal(ks[11], (DEPTH, SWA_HEADS), f32),
        'w_out': jax.random.normal(ks[12], (DEPTH, D_MIX, D_MODEL), f32) * D_MIX ** -0.5 * BETA,
        'ln_g': 1.0 + 0.02 * jax.random.normal(ks[13], (DEPTH, D_MODEL), f32),
        'ln_b': 0.02 * jax.random.normal(ks[14], (DEPTH, D_MODEL), f32),
    }

def reference(x, meta_tokens, ln0_g, ln0_b, rel_bias, w_in, b_f, mla_gq, mla_gkv, w_uq, w_ukv, sinks, w_out, ln_g, ln_b):
    B, S, D = x.shape
    lead = jnp.concatenate([jnp.zeros((B, PAD_LEAD, D), x.dtype),
                            jnp.broadcast_to(meta_tokens[None].astype(x.dtype), (B, N_META, D))], axis=1)
    h = jnp.concatenate([lead, x], axis=1)
    P = h.shape[1]
    pos = jnp.arange(P) - PAD_LEAD
    key_valid = pos >= 0
    top_k = min(TOPK_MAX, S // 4)
    h = layer_norm(h, ln0_g, ln0_b)
    for l in range(DEPTH):
        h = hybrid_layer(h, pos, key_valid, rel_bias, top_k, w_in[l], b_f[l], mla_gq[l], mla_gkv[l],
                         w_uq[l], w_ukv[l], sinks[l], w_out[l], ln_g[l], ln_b[l])
    return h[:, BLK:]


_drawn_inputs = setup_inputs


def setup_inputs(seed=0):
    import zlib

    import numpy as np

    out = dict(_drawn_inputs(seed))
    spreads = {}
    factors = {'meta_tokens': 8.0,
     'ln0_g': 2.778,
     'ln0_b': 2.973,
     'rel_bias': 8.0,
     'b_f': 8.0,
     'mla_gq': 8.0,
     'mla_gkv': 8.0,
     'w_uq': 6.925,
     'w_ukv': 4.798,
     'sinks': 8.0}
    for name, (base, spread) in spreads.items():
        noise = np.random.default_rng([zlib.crc32(name.encode()), seed]).standard_normal(out[name].shape)
        drawn = base * np.exp(spread * noise) if base else spread * noise
        out[name] = __import__('jax').numpy.asarray(drawn.astype(out[name].dtype))
    for name, factor in factors.items():
        out[name] = (out[name] * factor).astype(out[name].dtype)
    return out
```

```python
from contextlib import ExitStack

import concourse.bass as bass
from concourse import mybir

F32 = mybir.dt.float32
BF16 = mybir.dt.bfloat16
ALU = mybir.AluOpType
ACT = mybir.ActivationFunctionType
AX = mybir.AxisListType

D_MODEL, SEQ, DEPTH = 1024, 1024, 2
N_META, BLK = 16, 128
PAD = BLK - N_META
NB = SEQ // BLK + 1
NPAD = NB * BLK
NTOK = NPAD - PAD
KT = D_MODEL // BLK
HD, NH = 64, 8
ROPE = 32
Q_RANK, KV_RANK = 256, 128
TOPK = 256
ALPHA = (2 * DEPTH) ** 0.25
LN_EPS, RMS_EPS = 1e-5, 1e-6
NEG = -1e30
TAKEN = -3e38
A_SCALE = HD ** -0.5
B_SCALE = (HD + ROPE) ** -0.5
IW_SCALE = NH ** -0.5
CHUNKS = [(0, 348), (348, 348), (696, 344)]
LAG = 2
ORDER = [8, 7, 0, 2, 1, 4, 3, 6, 5]
MT_PER_LAYER = 40
LINE = 384
TOP_OPS = (NB - 2) * (TOPK // 4)


def keys_of(i):
    return N_META + BLK * i


def score_shape(br, i):
    n = keys_of(i)
    k0 = 0
    if br == "D" and i >= 2:
        k0, n = n - 2 * BLK, 2 * BLK
    nb = 1 if n <= 512 else (2 if n < 1024 else 4)
    bank = {8: 0, 7: 0, 6: 2, 5: 0, 4: 1 if br != "I" else 2, 3: 0, 2: 2 if br != "I" else 1, 1: 0, 0: 2}[i]
    return k0, n, nb, n // nb, bank


def key_slots(br, i):
    if br == "D":
        return [(0, 0)] if i == 0 else ([(i - 1, 9), (i, 7)] if i % 2 else [(i - 1, 7), (i, 8)])
    return [(k, 8 if (k == i and i and i % 2 == 0) else k) for k in range(i + 1)]


def pair_slots(br, a):
    if a == 0:
        return [(0, 0)]
    if br == "D":
        return [(2 * a - 2, 9), (2 * a - 1, 7), (2 * a, 8)]
    return [(k, k) for k in range(2 * a)] + [(2 * a, 8)]


class Plan:

    def __init__(self):
        self.items = []
        self.n = dict(pj=0, step=0, ix=0, tg=0, og=0, wt=0, ln=0, cum=0, ms=0, yy=0, pu=0, cn=0, pv=0, ds=0, pj_act=0, pj_dve=0)
        self.bank_owner = [None] * 4
        self.row_owner = [None] * 3
        self.hunit = 0
        self.ring = 0
        self.parts = {}
        self.xt_end = {}
        for b in range(NB):
            self.layer_norm(-1, b)
            if b:
                self.x_transpose(-1, b - 1)
        self.x_transpose(-1, NB - 1)
        for l in range(DEPTH):
            self.layer(l)

    def add(self, kind, **kw):
        kw["kind"] = kind
        kw["upto"] = dict(self.n)
        self.items.append(kw)
        return kw

    def take(self, key, k=1):
        v = self.n[key]
        self.n[key] += k
        return v

    def banks(self, which, event):
        old = [self.bank_owner[b] for b in which if self.bank_owner[b]]
        for b in which:
            self.bank_owner[b] = event
        return latest(old)

    def row(self, event):
        r = self.take("pu") % 3
        old = self.row_owner[r]
        self.row_owner[r] = event
        return r, latest([old] if old else [])

    def pj_groups(self, count, by="act", bank=None):
        out = []
        for _ in range(count):
            g, k = self.take("pj"), self.take("pj_" + by)
            c = bank
            if bank is None:
                c = self.ring
                self.ring = (self.ring + 1) % 4
            out.append((g, c, self.banks([c], ("pj_" + by, k + 1)), k + 1))
        return out

    def mt(self, l, what, **kw):
        self.part(l, self.take("wt"), what, [0, 1, 2], **kw)

    def part(self, l, wt, what, chunks, bank=None, **kw):
        self.parts[wt] = self.parts.get(wt, 0) + len(chunks)
        self.add("mt", l=l, what=what, wt=wt, chunks=[CHUNKS[c] for c in chunks], last=self.parts[wt] == 3,
                 groups=self.pj_groups(len(chunks), "dve" if what in ("G", "KR") else "act", bank), **kw)

    def tm(self, l, what):
        for b in range(NB):
            self.add("tm", l=l, what=what, b=b, groups=self.pj_groups(1), cn=NB * l + b)
            if what == "TB" and b:
                self.add("ct", l=l, b=b - 1, cn=NB * l + b - 1, tg=self.take("tg"))
        if what == "TB":
            self.add("ct", l=l, b=NB - 1, cn=NB * l + NB - 1, tg=self.take("tg"))

    def ms(self, l, what):
        self.add("ms", l=l, what=what, ms=self.take("ms"))

    def layer_norm(self, l, b):
        ln = self.take("ln")
        self.add("ln", l=l, b=b, ln=ln, xprev=self.xt_end.get(ln - 2))

    def x_transpose(self, l, b):
        ln = (l + 1) * NB + b
        tg = self.take("tg", 2)
        self.xt_end[ln] = tg + 2
        self.add("xt", l=l, b=b, ln=ln, tg=tg)

    def layer(self, l):
        self.ms(l, "start")
        self.tm(l, "TC")
        cum = self.take("cum")
        rows = [self.row(("cum_stored", 32 * (cum + 1))) for _ in range(2)]
        self.add("cum", l=l, cum=cum, rows=rows, waits=self.banks([0, 1, 2], ("cum_free", cum + 1)))
        self.mt(l, "IK")
        for p in range(4):
            self.mt(l, "IQ", p=p)
            for e in range(2):
                for i in range(2, NB):
                    ix = self.take("ix")
                    k0, n, nb, w, bank = score_shape("I", i)
                    waits = self.banks(range(bank, bank + nb), ("relu_done", ix + 1))
                    row, rwaits = self.row(("acc_done", ix + 1))
                    self.add("ix", l=l, p=p, e=e, i=i, ix=ix, n=n, nb=nb, w=w, bank=bank, waits=waits,
                             row=row, rwaits=rwaits, first=(p == 0 and e == 0), last=(p == 3 and e == 1))
        self.tm(l, "TA")
        self.ms(l, "A")
        self.pending, self.pv_next, self.rec_next = [], None, None
        for h in range(2):
            self.add("rows", l=l, h=h)
        self.mt(l, "AQK", h=0)
        for h in range(NH):
            self.head(l, "A", h)
            if h + 2 < NH:
                self.add("rows", l=l, h=h + 2)
        self.ms(l, "D")
        self.mt(l, "K", br="D")
        for h in range(NH):
            if h % 2 == 0:
                self.mt(l, "Q", br="D", p=h // 2)
            self.head(l, "D", h)
        self.flush()
        self.tm(l, "TB")
        self.add("uw", l=l)
        self.tm(l, "VB")
        self.mt(l, "KR")
        for h in range(NH):
            if h % 2 == 0:
                self.add("kb", l=l, p=h // 2, groups=self.pj_groups(3))
            self.add("qb", l=l, h=h, groups=self.pj_groups(3, "dve"))
            self.head(l, "B", h)
        self.ms(l, "C")
        self.mt(l, "K", br="C")
        for h in range(NH):
            if h % 2 == 0:
                self.mt(l, "Q", br="C", p=h // 2)
            self.head(l, "C", h)
        self.flush()
        self.add("wo", l=l)
        first = 0 if l < DEPTH - 1 else 1
        for b in range(first, NB):
            yy = self.take("yy")
            bank = 2 * (yy % 2)
            self.add("y", l=l, b=b, yy=yy, bank=bank, waits=self.banks([bank, bank + 1], ("y_free", yy + 1)),
                     first=(b == first))
            self.layer_norm(l, b)
            if l < DEPTH - 1 and b > first:
                self.x_transpose(l, b - 1)
        if l < DEPTH - 1:
            self.x_transpose(l, NB - 1)

    def lagged(self):
        s = self.pending.pop(0)
        self.add("tp", **s)
        self.values()
        if s["i"] % 2 or s["i"] == 0:
            self.pv_next = s

    def values(self):
        if self.pv_next:
            self.take("pv")
            self.add("pv", **self.pv_next)
            self.pv_next = None

    def normalise(self):
        if self.rec_next:
            self.add("rec", **self.rec_next)
            self.rec_next = None

    def flush(self):
        self.normalise()
        while self.pending:
            self.lagged()
        self.values()

    def head(self, l, br, h):
        hu = None
        if br in "CD":
            hu = self.hunit
            self.hunit += 1
        gwt = self.take("wt") if h % 2 == 0 else None
        nwt = self.take("wt") if br == "A" and h + 1 < NH else None
        for i in ORDER:
            step = self.take("step")
            k0, n, nb, w, bank = score_shape(br, i)
            waits = self.banks(range(bank, bank + nb), ("exp_done", step + 1))
            slots = key_slots(br, i)
            ntg = -(-len(slots) // 4)
            tg = self.take("tg", ntg)
            row, rwaits = self.row(("t_full", tg + ntg))
            a = (i + 1) // 2
            og = self.n["og"]
            if i % 2 or i == 0:
                self.take("og")
            s = dict(l=l, br=br, h=h, i=i, step=step, k0=k0, n=n, nb=nb, w=w, bank=bank, waits=waits,
                     slots=slots, tg=tg, ntg=ntg, row=row, rwaits=rwaits, a=a, og=og, hu=hu, ds=self.take("ds") if br == "D" else None)
            self.normalise()
            self.add("qk", **s)
            self.rec_next = s
            self.pending.append(s)
            if len(self.pending) > LAG:
                self.lagged()
            if gwt is not None and i in (0, 2):
                self.part(l, gwt, "G", [2 if i == 0 else 0], bank=3, br=br, p=h // 2)
            if nwt is not None and i == 4:
                self.part(l, nwt, "AQK", [0], bank=3, h=h + 1)
        self.ring = 2
        if gwt is not None:
            self.part(l, gwt, "G", [1], br=br, p=h // 2)
        if nwt is not None:
            self.part(l, nwt, "AQK", [1, 2], h=h + 1)


def latest(events):
    out = {}
    for name, v in events:
        out[name] = max(out.get(name, 0), v)
    return sorted(out.items())


def build(nc, t_in, out):
    plan = Plan()
    items = plan.items
    resid = [nc.dram_tensor(f"resid{l}", (NTOK, D_MODEL), F32, kind="Internal").ap() for l in range(DEPTH)]
    mixed = [nc.dram_tensor(f"mixed{l}", (16, BLK, NTOK), F32, kind="Internal").ap() for l in range(DEPTH)]
    lines = nc.dram_tensor("lines", (2 * NH, LINE), F32, kind="Internal")
    cumd = [nc.dram_tensor(f"cumd{l}", (2, NH, NPAD), F32, kind="Internal").ap() for l in range(DEPTH)]

    ctx = ExitStack()
    with ctx:
        def sb(name, shape, dt=F32):
            return ctx.enter_context(nc.sbuf_tensor(name, shape, dt))

        def sem(name):
            return ctx.enter_context(nc.semaphore(name))

        nV, nVC, nPT, nP, nW = NB * 512, NB * 256, 2 * 10 * 256, 3 * NPAD, 2 * KT * BLK
        arena = sb("arena", [BLK, nV + nVC + nPT + nP + nW])
        o = 0
        v_tok = arena[:, o:o + nV].rearrange("p (b c) -> p b c", b=NB); o += nV
        vc_tok = arena[:, o:o + nVC].rearrange("p (b c) -> p b c", b=NB); o += nVC
        probs_t = arena[:, o:o + nPT].rearrange("p (g s q) -> p g s q", g=2, s=10); o += nPT
        probs = arena[:, o:o + nP].rearrange("p (r k) -> p r k", r=3); o += nP
        w_ring = arena[:, o:o + nW].rearrange("p (s k c) -> p s k c", s=2, k=KT); o += nW
        w_out = arena[:, 0:16 * D_MODEL].rearrange("p (k n) -> p k n", k=16)
        qk = sb("qk", [BLK, 4 * NTOK])
        q_t = [qk[:, e * NTOK:(e + 1) * NTOK] for e in range(2)]
        k_t = [qk[:, (2 + e) * NTOK:(3 + e) * NTOK] for e in range(2)]
        mix_in = qk[:, 0:4096].rearrange("p (r k t) -> p r k t", r=2, k=16)
        vw = sb("vw", [BLK, KT * 512])
        u_q = vw[:, 0:2048].rearrange("p (k c) -> p k c", k=2)
        u_k = vw[:, 2048:2560]
        u_v = vw[:, 2560:3072]
        ln_g, ln_b = vw[:, 0:1024], vw[:, 1024:2048]
        z_sum = vw[:, 2048:4096].rearrange("p (r n) -> p r n", r=2)
        s_off = {}
        so = 0
        for i in range(2, NB):
            s_off[i] = so
            so += keys_of(i)
        score = sb("score", [BLK, so])
        res_in = score[:, 0:2048].rearrange("p (r n) -> p r n", r=2)
        x_new = score[:, 2048:4096].rearrange("p (r n) -> p r n", r=2)
        xT = sb("xT", [BLK, KT, NPAD])
        cT = sb("cT", [BLK, 3, NPAD])
        sel = sb("sel", [BLK, so], BF16)
        gate = sb("gate", [BLK, NTOK])
        mixg = sb("mixg", [BLK, 4, 256])
        hankel = sb("hankel", [BLK, 2, 256])
        rope_t = sb("rope_t", [BLK, NTOK])
        cn = sb("cn", [BLK, 2, Q_RANK + KV_RANK])
        ident = sb("ident", [BLK, BLK])
        anti = sb("anti", [BLK, BLK])
        ident_b = sb("ident_b", [BLK, BLK], BF16)
        tri_b = sb("tri_b", [BLK, BLK], BF16)
        upper1 = sb("upper1", [BLK, 4 * BLK])
        rel = sb("rel", [32, 2 * NH])
        onehot = cT[0:32, 1, 0:2 * LINE]
        lmask = cT[0:NH, 0, 0:2 * LINE]
        line_sb = cT[0:NH, 2, 0:2 * LINE]
        small = sb("small", [BLK, 256])
        rowmask = small[:, 0:1]
        halfneg = small[:, 1:2]
        gq = small[:, 2:2 + 2 * DEPTH]
        gkv = small[:, 6:6 + DEPTH]
        sink = small[:, 8:8 + DEPTH * NH]
        nsink = small[:, 24:24 + DEPTH * NH]
        nmax = small[:, 40:44]
        psums = small[:, 44:48]
        rinv = small[:, 48:52]
        esink = small[:, 52:56]
        stats = small[:, 56:80].rearrange("p (r c) -> p r c", r=2)
        mv = small[:, 80:84].rearrange("p (r c) -> p r c", r=2)
        rstd = small[:, 84:88].rearrange("p (r c) -> p r c", r=2)
        top8 = small[:, 88:96]
        cstat = small[:, 96:100].rearrange("p (r c) -> p r c", r=2)
        crs = small[:, 100:104].rearrange("p (r c) -> p r c", r=2)
        iws = small[:, 104:176].rearrange("p (b h) -> p b h", b=NB)
        bf = sb("bf", [BLK, DEPTH * 72])
        fz = sb("fz", [BLK, NB, 16])
        fw = cT[:, 0, 0:6 * 72].rearrange("p (a b) -> p a b", a=6)
        f3 = [fw[:, j, :].rearrange("p (b h) -> p b h", b=NB) for j in range(6)]
        squares = sb("squares", [BLK, Q_RANK], BF16)

        ps_s = ctx.enter_context(nc.psum_tensor("ps_s", [BLK, 4, 512], F32))
        ps_t = ctx.enter_context(nc.psum_tensor("ps_t", [BLK, 2, 512], F32))
        ps_o = ctx.enter_context(nc.psum_tensor("ps_o", [BLK, 2, 512], F32))
        rtmp = sb("rtmp", [BLK, 348])

        names = """pj_full pj_act pj_dve s_full relu_full relu_done acc_done max_done exp_done es_done 
                   nrm_done t_full t_free pv_done o_free y_full y_free cum_in cum_full cum_free cum_stored
                   ms_done mask_done ln_var ln_rs ln_done dve_chain pool_chain act_chain half_done gate_in
                   cn_raw cn_rs cn_done consts line_full line_ready line_stored lnp_ld fe_in fe_out top_step
                   zero_done small_done""".split()
        S = {n: sem(n) for n in names}
        w_ld = [sem(f"w_ld{i}") for i in range(2)]
        h_ld = [sem(f"h_ld{i}") for i in range(2)]
        mx_st = [sem(f"mx_st{i}") for i in range(4)]
        mb_ld = [sem(f"mb_ld{i}") for i in range(2)]
        r_ld = [sem(f"r_ld{i}") for i in range(2)]
        x_st = [sem(f"x_st{i}") for i in range(2)]
        row_ld = [sem(f"row_ld{i}") for i in range(2)]
        vw_ld = sem("vw_ld")
        wo_ld = [sem(f"wo_ld{i}") for i in range(4)]
        block = ctx.enter_context(nc.Block())

        def vw_need(l, what):
            return 16 * (6 * l + {"TC": 1, "TA": 2, "TB": 3, "VB": 6}[what])

        w_used, vw_used, head_end, head_of, a_end = {}, {}, {}, {}, {}
        for it in items:
            if it["kind"] == "mt":
                w_used[it["wt"]] = it["groups"][-1][0] + 1
            if it["kind"] == "tm":
                vw_used[(it["l"], it["what"])] = it["groups"][-1][0] + 1
            if it["kind"] == "qb":
                vw_used[(it["l"], "U")] = it["groups"][-1][0] + 1
            if it["kind"] == "qk":
                if it["hu"] is not None:
                    head_end[it["hu"]] = it["step"] + 1
                    head_of[it["hu"]] = (it["l"], it["br"], it["h"])
                if it["br"] == "A":
                    a_end[(it["l"], it["h"])] = it["step"] + 1

        ct_end = {it["cn"]: it["tg"] + 1 for it in items if it["kind"] == "ct"}
        c_end = {it["l"]: it["step"] + 1 for it in items if it["kind"] == "qk" and it["br"] == "C"}
        gate_ready, at = {}, 0
        for it in items:
            if it["kind"] == "mt" and it["what"] == "G":
                at = it["groups"][-1][3]
            if it["kind"] == "pv":
                gate_ready[it["og"]] = at
        gcount, hcount = [0], [0]
        f_tmp = cT[:, 0, 1024:1152]

        def ln_rows(b):
            return N_META if b == 0 else BLK

        def tok0(b):
            return 0 if b == 0 else N_META + BLK * (b - 1)

        def col0(b):
            return PAD if b == 0 else BLK * b

        def waits(eng, pairs):
            for name, v in pairs:
                eng.wait_ge(S[name], v)

        def k_index(br, h):
            return h % 2 if br in "AB" else h // (NH // 2)

        def lnset(l):
            return l + 1

        @block.sync
        def _(sp):
            for dst, src in ((ident, "ident"), (anti, "anti"), (upper1, "upper1"), (rel, "rel_bias"),
                             (rope_t, "rope_t"), (bf, "b_f")):
                sp.dma_start(dst[:], t_in[src]).then_inc(S["consts"], 16)
            sp.dma_start(onehot, t_in["onehot"]).then_inc(S["consts"], 16)
            sp.dma_start(lmask, t_in["lmask"]).then_inc(S["consts"], 16)
            sp.dma_start(small[:, 0:24], t_in["small"]).then_inc(S["consts"], 16)

            def load_ln(l):
                sp.dma_start(ln_g, t_in["ln_g"][lnset(l)]).then_inc(S["lnp_ld"], 16)
                sp.dma_start(ln_b, t_in["ln_b"][lnset(l)]).then_inc(S["lnp_ld"], 16)

            def store_lines():
                sp.wait_ge(S["line_ready"], 1)
                for j in range(2):
                    sp.dma_start(lines.ap()[NH * j:NH * (j + 1), :], line_sb[:, LINE * j:LINE * (j + 1)]
                                 ).then_inc(S["line_stored"], 16)

            def load_w(wt):
                if wt >= DEPTH * MT_PER_LAYER:
                    return
                if wt >= 2:
                    sp.wait_ge(S["pj_full"], w_used[wt - 2])
                sp.dma_start(w_ring[:, wt % 2], t_in["w_feat"][wt // MT_PER_LAYER, wt % MT_PER_LAYER]
                             ).then_inc(w_ld[wt % 2], 16)

            def load_hankel(hu):
                if hu >= 2 * DEPTH * NH:
                    return
                if hu >= 2:
                    sp.wait_ge(S["s_full"], head_end[hu - 2])
                l, br, h = head_of[hu]
                src = bass.AP(lines, ((0 if br == "C" else NH) + h) * LINE, [[1, BLK], [1, 256]])
                sp.dma_start(hankel[:, hu % 2, :], src).then_inc(h_ld[hu % 2], 16)

            load_ln(-1)
            x_dram = t_in["x"]
            store_lines()
            for it in items:
                kind, l = it["kind"], it["l"]
                if kind == "ln":
                    ln, b = it["ln"], it["b"]
                    M = ln_rows(b)
                    if l < 0:
                        if ln >= 2:
                            sp.wait_ge(S["ln_done"], ln - 1)
                        src = t_in["meta_tokens"] if b == 0 else x_dram[0, BLK * (b - 1):BLK * b, :]
                        sp.dma_start(res_in[0:M, ln % 2, :], src).then_inc(r_ld[ln % 2], 16)
                    done = [(ln - 1, b - 1)] if b > (1 if l == DEPTH - 1 else 0) else []
                    if b == NB - 1:
                        done.append((ln, b))
                    for n, c in done:
                        sp.wait_ge(S["ln_done"], n + 1)
                        M = ln_rows(c)
                        dst = resid[l + 1][tok0(c):tok0(c) + M, :] if l < DEPTH - 1 else out[0, BLK * (c - 1):BLK * c, :]
                        sp.dma_start(dst, x_new[0:M, n % 2, :]).then_inc(x_st[n % 2], 16)
                if kind == "ms" and it["what"] == "start":
                    sp.wait_ge(S["ln_done"], it["upto"]["ln"])
                    sp.wait_ge(S["y_free"], it["upto"]["yy"]) if l > 0 else None
                    sp.dma_start(vw[:, 0:KT * 272], t_in["w_tc"][l]).then_inc(vw_ld, 16)
                    if l > 0:
                        sp.wait_ge(S["y_full"], it["upto"]["yy"])
                    for j in range(2):
                        wt = it["upto"]["wt"] + j
                        sp.dma_start(w_ring[:, wt % 2], t_in["w_feat"][l, j]).then_inc(w_ld[wt % 2], 16)
                if kind == "cum":
                    sp.wait_ge(S["pj_full"], vw_used[(l, "TC")])
                    sp.dma_start(vw[:, 0:KT * 512], t_in["w_ta"][l]).then_inc(vw_ld, 16)
                    sp.wait_ge(S["cum_free"], it["cum"] + 1)
                    for j in range(2):
                        sp.dma_start(cumd[l][j], probs[0:NH, it["rows"][j][0], :]).then_inc(S["cum_stored"], 16)
                if kind == "ms" and it["what"] == "A":
                    sp.wait_ge(S["ms_done"], it["ms"] + 1)
                    sp.wait_ge(S["cum_stored"], 32 * (l + 1))
                    sp.wait_ge(S["pj_full"], vw_used[(l, "TA")])
                    sp.dma_start(vw[:, 0:KT * 384], t_in["w_tb"][l]).then_inc(vw_ld, 16)
                    if l == 0:
                        sp.wait_ge(S["line_stored"], 32)
                        for hu in range(2):
                            load_hankel(hu)
                if kind == "rows":
                    h = it["h"]
                    if h >= 2:
                        sp.wait_ge(S["s_full"], a_end[(l, h - 2)])
                    sp.dma_start(q_t[h % 2][HD + 1:HD + 2, :], cumd[l][0, h:h + 1, PAD:]).then_inc(row_ld[h % 2], 16)
                    sp.dma_start(k_t[h % 2][HD:HD + 1, :], cumd[l][1, h:h + 1, PAD:]).then_inc(row_ld[h % 2], 16)
                if kind == "mt" and it["last"] and (it["wt"] % MT_PER_LAYER) < MT_PER_LAYER - 2:
                    load_w(it["wt"] + 2)
                if kind == "uw":
                    sp.wait_ge(S["pj_full"], vw_used[(l, "TB")])
                    sp.dma_start(vw[:, 0:2048], t_in["u_q"][l]).then_inc(vw_ld, 16)
                    sp.dma_start(u_k, t_in["u_k"][l]).then_inc(vw_ld, 16)
                    sp.dma_start(u_v, t_in["u_v"][l]).then_inc(vw_ld, 16)
                if kind == "pv":
                    og, a = it["og"], it["a"]
                    r0 = HD * (it["h"] % 2)
                    c0, w = (0, N_META) if a == 0 else (N_META + 256 * (a - 1), 256)
                    tile = "ABCD".index(it["br"]) * 4 + it["h"] // 2
                    sp.wait_ge(S["o_free"], og + 1)
                    sp.dma_start(mixed[l][tile, r0:r0 + HD, c0:c0 + w], mixg[r0:r0 + HD, og % 4, 0:w]
                                 ).then_inc(mx_st[og % 4], 16)
                if kind == "qk" and it["hu"] is not None and it["i"] == NB - 1 and it["hu"] >= 1:
                    load_hankel(it["hu"] + 1)
                if kind == "wo":
                    sp.wait_ge(S["pv_done"], it["upto"]["pv"])
                    load_ln(l)
                    for j in range(4):
                        sp.dma_start(w_out[:, 4 * j:4 * j + 4, :], t_in["w_out"][l, :, 4 * j:4 * j + 4, :]
                                     ).then_inc(wo_ld[j], 16)
                    for j in range(4):
                        sp.wait_ge(mx_st[j], 16 * len([g for g in range(it["upto"]["og"]) if g % 4 == j]))
                    for j in range(2):
                        sp.wait_ge(x_st[j], 16 * len([n for n in range(it["upto"]["ln"]) if n % 2 == j]))
                if kind == "y":
                    yy, b, ln = it["yy"], it["b"], it["upto"]["ln"]
                    M = ln_rows(b)
                    if yy >= 2:
                        sp.wait_ge(S["y_full"], yy - 1)
                    sp.wait_ge(S["ln_done"], ln - 1)
                    sp.dma_start(mix_in[:, yy % 2, :, 0:M], mixed[l][:, :, tok0(b):tok0(b) + M]
                                 .rearrange("k p t -> p k t")).then_inc(mb_ld[yy % 2], 16)
                    sp.dma_start(res_in[0:M, ln % 2, :], resid[l][tok0(b):tok0(b) + M, :]).then_inc(r_ld[ln % 2], 16)
            for j in range(2):
                sp.wait_ge(x_st[j], 16 * len([n for n in range(plan.n["ln"]) if n % 2 == j]))

        @block.tensor
        def _(pe):
            pe.wait_ge(S["consts"], 16 * 9)
            pe.wait_ge(S["small_done"], 1)
            pe.matmul(ps_o[0:NH, 0, 0:LINE], rel[:, 0:NH], onehot[:, 0:LINE], start=True, stop=True)
            pe.matmul(ps_o[0:NH, 1, 0:LINE], rel[:, NH:2 * NH], onehot[:, LINE:2 * LINE],
                      start=True, stop=True).then_inc(S["line_full"], 1)
            for it in items:
                kind, l = it["kind"], it["l"]
                if kind == "xt":
                    M = ln_rows(it["b"])
                    pe.wait_ge(S["ln_done"], it["ln"] + 1)
                    for j in range(2):
                        tg = it["tg"] + j
                        if tg >= 2:
                            pe.wait_ge(S["t_free"], tg - 1)
                        for c in range(4):
                            k = 4 * j + c
                            mm = pe.transpose(ps_t[:, tg % 2, c * BLK:c * BLK + M],
                                              x_new[0:M, it["ln"] % 2, k * BLK:(k + 1) * BLK], ident[0:M, 0:M])
                        mm.then_inc(S["t_full"], 1)
                elif kind == "tm":
                    b, what = it["b"], it["what"]
                    g, bank, free, _ = it["groups"][0]
                    if b == 0:
                        pe.wait_ge(vw_ld, vw_need(l, what))
                        pe.wait_ge(S["t_free"], it["upto"]["tg"])
                    waits(pe, free)
                    if what == "VB":
                        mm = pe.matmul(ps_s[:, bank, 0:512], cT[:, 2, b * BLK:(b + 1) * BLK], u_v,
                                       start=True, stop=True)
                    else:
                        n = {"TC": 272, "TA": 512, "TB": 384}[what]
                        wv = vw[:, 0:KT * n].rearrange("p (k n) -> p k n", k=KT)
                        for k in range(KT):
                            mm = pe.matmul(ps_s[:, bank, 0:n], xT[:, k, b * BLK:(b + 1) * BLK], wv[:, k, :],
                                           start=(k == 0), stop=(k == KT - 1))
                    mm.then_inc(S["pj_full"], 1)
                elif kind == "ct":
                    tg = it["tg"]
                    pe.wait_ge(S["cn_done"], it["cn"] + 1)
                    pe.wait_ge(S["t_free"], tg - 1)
                    for j in range(3):
                        mm = pe.transpose(ps_t[:, tg % 2, j * BLK:(j + 1) * BLK],
                                          cn[:, it["cn"] % 2, j * BLK:(j + 1) * BLK], ident[:])
                    mm.then_inc(S["t_full"], 1)
                elif kind == "cum":
                    pe.wait_ge(S["cum_in"], it["cum"] + 1)
                    waits(pe, it["waits"])
                    for c in range(3):
                        for b in range(3 * c + 3):
                            j = max(b - 3 * c, 0)
                            src = upper1[:, 0:(3 - j) * BLK] if b >= 3 * c else upper1[:, BLK:4 * BLK]
                            mm = pe.matmul(ps_s[0:NH, c, j * BLK:3 * BLK], f3[5][:, b, :], src,
                                           start=(b == 0), stop=True, skip_group_check=(b > 0))
                    mm.then_inc(S["cum_full"], 1)
                elif kind == "mt":
                    wt = it["wt"]
                    pe.wait_ge(w_ld[wt % 2], 16 * (wt // 2 + 1))
                    for (g, bank, free, _), (c0, w) in zip(it["groups"], it["chunks"]):
                        waits(pe, free)
                        for k in range(KT):
                            mm = pe.matmul(ps_s[:, bank, 0:w], w_ring[:, wt % 2, k, :],
                                           xT[:, k, PAD + c0:PAD + c0 + w], start=(k == 0), stop=(k == KT - 1))
                        mm.then_inc(S["pj_full"], 1)
                elif kind == "qb":
                    for (g, bank, free, _), (c0, w) in zip(it["groups"], CHUNKS):
                        waits(pe, free)
                        for k in range(2):
                            mm = pe.matmul(ps_s[:, bank, 0:w], u_q[:, k, it["h"] * BLK:(it["h"] + 1) * BLK],
                                           cT[:, k, PAD + c0:PAD + c0 + w], start=(k == 0), stop=(k == 1))
                        mm.then_inc(S["pj_full"], 1)
                elif kind == "kb":
                    for (g, bank, free, _), (c0, w) in zip(it["groups"], CHUNKS):
                        waits(pe, free)
                        pe.matmul(ps_s[:, bank, 0:w], u_k[:, it["p"] * BLK:(it["p"] + 1) * BLK],
                                  cT[:, 2, PAD + c0:PAD + c0 + w], start=True, stop=True).then_inc(S["pj_full"], 1)
                elif kind == "ix":
                    i, w = it["i"], it["w"]
                    if i == 2:
                        waits(pe, [(n, it["upto"][n]) for n in ("pj_act", "pj_dve") if it["upto"][n]])
                        pe.wait_ge(S["ms_done"], it["upto"]["ms"])
                    waits(pe, it["waits"])
                    q0 = tok0(i)
                    for c in range(it["nb"]):
                        mm = pe.matmul(ps_s[:, it["bank"] + c, 0:w], q_t[it["p"] % 2][:, q0:q0 + BLK],
                                       k_t[it["e"]][:, c * w:(c + 1) * w], start=True, stop=True)
                    mm.then_inc(S["relu_full"], 1)
                elif kind == "qk":
                    br, h, i, w, nb = it["br"], it["h"], it["i"], it["w"], it["nb"]
                    M, r0 = (N_META, PAD) if i == 0 else (BLK, 0)
                    if i == NB - 1:
                        waits(pe, [(n, it["upto"][n]) for n in ("pj_act", "pj_dve") if it["upto"][n]])
                        pe.wait_ge(S["ms_done"], it["upto"]["ms"])
                        if br == "A":
                            pe.wait_ge(row_ld[h % 2], 32 * (NH // 2 * l + h // 2 + 1))
                        if it["hu"] is not None:
                            pe.wait_ge(h_ld[it["hu"] % 2], 16 * (it["hu"] // 2 + 1))
                    if br == "C" and h == 0 and i >= 2:
                        pe.wait_ge(S["mask_done"], 7 * l + (NB - i))
                    waits(pe, it["waits"])
                    qh = q_t[h % 2][:, tok0(i):tok0(i) + M]
                    kh = k_t[k_index(br, h)]
                    for c in range(nb):
                        dst = ps_s[0:M, it["bank"] + c, 0:w]
                        extra = []
                        if br == "C" and i >= 2:
                            m0 = s_off[i] + c * w
                            extra.append((dst, ident_b[:, r0:r0 + M], sel[:, m0:m0 + w]))
                        if c == nb - 1:
                            if br in "AB" or (br == "C" and i < 2):
                                extra.append((dst[:, w - min(w, M):w], ident_b[:, r0:r0 + M], tri_b[:, r0:BLK]))
                            if br in "CD":
                                wd = min(it["n"], 256)
                                extra.append((dst[:, w - wd:w], anti[:, r0:r0 + M],
                                              hankel[:, it["hu"] % 2, 256 - wd:256]))
                        mm = pe.matmul(dst, qh, kh[:, it["k0"] + c * w:it["k0"] + (c + 1) * w],
                                       start=True, stop=True)
                        for j, (d2, lhs, rhs) in enumerate(extra):
                            mm = pe.matmul(d2, lhs, rhs, start=False, stop=True, skip_group_check=True)
                    mm.then_inc(S["s_full"], 1)
                elif kind == "tp":
                    M = ln_rows(it["i"])
                    pe.wait_ge(S["nrm_done"], it["step"] + 1)
                    for j in range(it["ntg"]):
                        tg = it["tg"] + j
                        pe.wait_ge(S["t_free"], tg - 1)
                        for c, (kb, _) in enumerate(it["slots"][4 * j:4 * j + 4]):
                            mm = pe.transpose(ps_t[:, tg % 2, c * BLK:c * BLK + M],
                                              probs[0:M, it["row"], kb * BLK:(kb + 1) * BLK], ident[0:M, 0:M])
                        mm.then_inc(S["t_full"], 1)
                elif kind == "pv":
                    br, h, a, og = it["br"], it["h"], it["a"], it["og"]
                    pe.wait_ge(S["t_free"], it["tg"] + it["ntg"])
                    if og >= 2:
                        pe.wait_ge(S["o_free"], og - 1)
                    w = N_META if a == 0 else 256
                    r0 = HD * (h % 2)
                    src = pair_slots(br, a)
                    for j, (kb, slot) in enumerate(src):
                        if br in "AB":
                            v = v_tok[:, kb, h * HD:(h + 1) * HD]
                        else:
                            c0 = (0 if br == "C" else 128) + HD * (h // (NH // 2))
                            v = vc_tok[:, kb, c0:c0 + HD]
                        mm = pe.matmul(ps_o[r0:r0 + HD, og % 2, 0:w], v, probs_t[:, og % 2, slot, 0:w],
                                       start=(j == 0), stop=(j == len(src) - 1))
                    mm.then_inc(S["pv_done"], 1)
                elif kind == "y":
                    yy, bank = it["yy"], it["bank"]
                    M = ln_rows(it["b"])
                    pe.wait_ge(mb_ld[yy % 2], 16 * (yy // 2 + 1))
                    waits(pe, it["waits"])
                    for half in range(2):
                        for k in range(16):
                            if it["first"] and half == 0 and k % 4 == 0:
                                pe.wait_ge(wo_ld[k // 4], 16 * (l + 1))
                            mm = pe.matmul(ps_s[0:M, bank + half, :], mix_in[:, yy % 2, k, 0:M],
                                           w_out[:, k, half * 512:(half + 1) * 512],
                                           start=(k == 0), stop=(k == 15))
                    mm.then_inc(S["y_full"], 1)


        @block.scalar
        def _(act):
            chain = [0]

            def link(ins):
                chain[0] += 1
                ins.then_inc(S["act_chain"], 1)
                act.wait_ge(S["act_chain"], chain[0])

            act.wait_ge(S["consts"], 16 * 9)
            for it in items:
                kind, l = it["kind"], it["l"]
                if kind == "xt":
                    b = it["b"]
                    M = ln_rows(b)
                    for j in range(2):
                        tg = it["tg"] + j
                        act.wait_ge(S["t_full"], tg + 1)
                        src = ps_t[:, tg % 2, :].rearrange("p (c t) -> p c t", c=4)[:, :, 0:M]
                        nc.scalar.activation(xT[:, 4 * j:4 * j + 4, col0(b):col0(b) + M], src,
                                             ACT.Copy).then_inc(S["t_free"], 1)
                elif kind == "tm":
                    b, what = it["b"], it["what"]
                    g, bank, _, nth = it["groups"][0]
                    act.wait_ge(S["pj_full"], g + 1)
                    if what == "TC":
                        nc.scalar.activation(vc_tok[:, b, :], ps_s[:, bank, 0:256], ACT.Copy)
                        nc.scalar.activation(fz[:, b, :], ps_s[:, bank, 256:272], ACT.Copy).then_inc(S["pj_act"], 1)
                    elif what in ("TA", "VB"):
                        nc.scalar.activation(v_tok[:, b, :], ps_s[:, bank, :], ACT.Copy).then_inc(S["pj_act"], 1)
                    else:
                        c = it["cn"]
                        if c >= 2:
                            act.wait_ge(S["t_full"], ct_end[c - 2])
                        if b == 0:
                            act.wait_ge(S["line_stored"], 32)
                        nc.scalar.activation(cn[:, c % 2, :], ps_s[:, bank, 0:384], ACT.Copy)
                        link(nc.scalar.activation(squares[:, 0:Q_RANK], ps_s[:, bank, 0:Q_RANK], ACT.Square,
                                                  accum_out=cstat[:, c % 2, 0:1]))
                        nc.scalar.activation(squares[:, 0:KV_RANK], ps_s[:, bank, Q_RANK:384], ACT.Square,
                                             accum_out=cstat[:, c % 2, 1:2]).then_inc(S["pj_act"], 1)
                        act.wait_ge(S["pj_act"], nth)
                elif kind == "ct":
                    tg, b = it["tg"], it["b"]
                    act.wait_ge(S["t_full"], tg + 1)
                    for j in range(3):
                        gain = gq[:, 2 * l + j:2 * l + j + 1] if j < 2 else gkv[:, l:l + 1]
                        a = nc.scalar.activation(cT[:, j, b * BLK:(b + 1) * BLK], ps_t[:, tg % 2, j * BLK:(j + 1) * BLK],
                                                 ACT.Copy, scale=gain)
                    a.then_inc(S["t_free"], 1)
                elif kind == "cum":
                    act.wait_ge(S["fe_in"], it["cum"] + 1)
                    nc.scalar.activation(fw[:, 2, :], fw[:, 1, :], ACT.Exp, scale=-1.0).then_inc(S["fe_out"], 1)
                    act.wait_ge(S["cum_full"], it["cum"] + 1)
                    for j, (row, rw) in enumerate(it["rows"]):
                        waits(act, rw)
                        a = nc.scalar.activation(probs[0:NH, row, :].rearrange("p (c t) -> p c t", c=3),
                                                 ps_s[0:NH, 0:3, 0:3 * BLK], ACT.Copy, scale=(1.0, -1.0)[j])
                    a.then_inc(S["cum_free"], 1)
                elif kind == "mt":
                    what = it["what"]
                    for (g, bank, _, nth), (c0, w) in zip(it["groups"], it["chunks"]):
                        act.wait_ge(S["pj_full"], g + 1)
                        ps = ps_s[:, bank, 0:w]
                        cs = slice(c0, c0 + w)
                        done = S["pj_act"]
                        if what == "IK":
                            act.wait_ge(S["ms_done"], it["upto"]["ms"])
                            nc.scalar.activation(k_t[0][0:HD, cs], ps[0:HD], ACT.Copy)
                            a = nc.scalar.activation(k_t[1][HD:BLK, cs], ps[HD:BLK], ACT.Copy)
                        elif what == "IQ":
                            a = nc.scalar.activation(q_t[it["p"] % 2][:, cs], ps, ACT.Copy, scale=A_SCALE)
                        elif what == "AQK":
                            h = it["h"]
                            nc.scalar.activation(q_t[h % 2][0:HD, cs], ps[0:HD], ACT.Copy, scale=A_SCALE)
                            a = nc.scalar.activation(k_t[h % 2][0:HD, cs], ps[HD:BLK], ACT.Copy)
                        elif what in "QK":
                            dst, sc = (q_t, A_SCALE) if what == "Q" else (k_t, 1.0)
                            nc.scalar.activation(dst[0][0:HD, cs], ps[0:HD], ACT.Copy, scale=sc)
                            a = nc.scalar.activation(dst[1][0:HD, cs], ps[HD:BLK], ACT.Copy, scale=sc)
                        elif what == "G":
                            if it["upto"]["pv"]:
                                act.wait_ge(S["o_free"], it["upto"]["pv"])
                            a = nc.scalar.activation(gate[:, cs], ps, ACT.Tanh, scale=0.5)
                            done = S["gate_in"]
                        elif what == "KR":
                            continue
                        a.then_inc(done, 1)
                elif kind == "kb":
                    for (g, bank, _, nth), (c0, w) in zip(it["groups"], CHUNKS):
                        act.wait_ge(S["pj_full"], g + 1)
                        nc.scalar.activation(k_t[0][0:HD, c0:c0 + w], ps_s[0:HD, bank, 0:w], ACT.Copy)
                        nc.scalar.activation(k_t[1][0:HD, c0:c0 + w], ps_s[HD:BLK, bank, 0:w],
                                             ACT.Copy).then_inc(S["pj_act"], 1)
                elif kind == "qb":
                    for (g, bank, _, nth), (c0, w) in zip(it["groups"], CHUNKS):
                        act.wait_ge(S["pj_full"], g + 1)
                        nc.scalar.activation(q_t[it["h"] % 2][0:HD, c0:c0 + w], ps_s[0:HD, bank, 0:w], ACT.Copy,
                                             scale=B_SCALE).then_inc(S["half_done"], 1)
                elif kind == "ix":
                    act.wait_ge(S["relu_full"], it["ix"] + 1)
                    waits(act, it["rwaits"])
                    dst = probs[:, it["row"], PAD:PAD + it["n"]].rearrange("p (c t) -> p c t", c=it["nb"])
                    nc.scalar.activation(dst, ps_s[:, it["bank"]:it["bank"] + it["nb"], 0:it["w"]],
                                         ACT.Relu).then_inc(S["relu_done"], 1)
                elif kind == "qk":
                    br, i, step = it["br"], it["i"], it["step"]
                    M = ln_rows(i)
                    act.wait_ge(S["max_done"], step + 1)
                    waits(act, it["rwaits"])
                    if br == "D":
                        s0 = NH * l + it["h"]
                        nc.scalar.activation(esink[0:M, step % 4:step % 4 + 1], sink[0:M, s0:s0 + 1], ACT.Exp,
                                             bias=nmax[0:M, step % 4:step % 4 + 1]).then_inc(S["es_done"], 1)
                    off = p_off(br, i)
                    dst = probs[0:M, it["row"], off:off + it["n"]].rearrange("p (c t) -> p c t", c=it["nb"])
                    nc.scalar.activation(dst, ps_s[0:M, it["bank"]:it["bank"] + it["nb"], 0:it["w"]], ACT.Exp,
                                         bias=nmax[0:M, step % 4:step % 4 + 1],
                                         accum_out=psums[0:M, step % 4:step % 4 + 1]).then_inc(S["exp_done"], 1)
                elif kind == "tp":
                    i, og = it["i"], it["og"]
                    M = ln_rows(i)
                    c0 = BLK if (i and i % 2 == 0) else 0
                    if og >= 2:
                        act.wait_ge(S["pv_done"], og - 1)
                    act.wait_ge(S["ms_done"], it["upto"]["ms"])
                    for j in range(it["ntg"]):
                        tg = it["tg"] + j
                        act.wait_ge(S["t_full"], tg + 1)
                        for c, slot, k in runs([s for _, s in it["slots"][4 * j:4 * j + 4]]):
                            src = ps_t[:, tg % 2, c * BLK:(c + k) * BLK].rearrange("p (k t) -> p k t", k=k)[:, :, 0:M]
                            a = nc.scalar.activation(probs_t[:, og % 2, slot:slot + k, c0:c0 + M], src, ACT.Copy)
                        a.then_inc(S["t_free"], 1)

        @block.vector
        def _(dve):
            chain = [0]

            def link(ins):
                chain[0] += 1
                ins.then_inc(S["dve_chain"], 1)
                dve.wait_ge(S["dve_chain"], chain[0])

            dve.wait_ge(S["consts"], 16 * 9)
            dve.tensor_copy(ident_b[:], ident[:])
            link(dve.tensor_tensor(f_tmp, upper1[:, 0:BLK], ident[:], ALU.subtract))
            dve.tensor_scalar(tri_b[:], f_tmp, NEG, None, ALU.mult)
            dve.tensor_scalar(nsink, sink, -1.0, None, ALU.mult).then_inc(S["small_done"], 1)
            dve.wait_ge(S["line_full"], 1)
            dve.tensor_tensor(line_sb, ps_o[0:NH, :, 0:LINE], lmask, ALU.add).then_inc(S["line_ready"], 1)

            top = {"next": TOP_OPS}

            def top_ops(l, count):
                for _ in range(count):
                    if top["next"] >= TOP_OPS:
                        return
                    i, r = NB - 1 - top["next"] // (TOPK // 4), top["next"] % (TOPK // 4)
                    top["next"] += 1
                    n = keys_of(i)
                    sc = score[:, s_off[i]:s_off[i] + n]
                    if r:
                        dve.wait_ge(S["top_step"], top["steps"])
                    if r % 2 == 0:
                        dve.max(top8, sc).then_inc(S["top_step"], 1)
                    else:
                        dve.match_replace(sc, top8, sc, TAKEN).then_inc(S["top_step"], 1)
                    top["steps"] = top.get("steps", 0) + 1
                    if r == TOPK // 4 - 1:
                        dve.wait_ge(S["top_step"], top["steps"])
                        m = sel[:, s_off[i]:s_off[i] + n]
                        if l > 0 and i == NB - 1:
                            dve.wait_ge(S["s_full"], c_end[l - 1])
                        link(dve.tensor_scalar(m, sc, TAKEN, NEG, ALU.is_gt, ALU.mult))
                        dve.tensor_tensor(m[:, n - BLK:n], m[:, n - BLK:n], tri_b[:], ALU.min
                                          ).then_inc(S["mask_done"], 1)

            for it in items:
                kind, l = it["kind"], it["l"]
                if kind == "ln":
                    ln, b = it["ln"], it["b"]
                    M, r = ln_rows(b), ln % 2
                    if b == 0 or (l == DEPTH - 1 and b == 1):
                        dve.wait_ge(S["lnp_ld"], 32 * (l + 2))
                        if l >= 0:
                            dve.wait_ge(S["pj_full"], vw_used[(l, "U")])
                    dve.wait_ge(r_ld[r], 16 * (ln // 2 + 1))
                    z = res_in[0:M, r, :]
                    if l >= 0:
                        dve.wait_ge(S["y_full"], it["upto"]["yy"])
                        bank = 2 * ((it["upto"]["yy"] - 1) % 2)
                        z = z_sum[0:M, r, :]
                        dve.scalar_tensor_tensor(z, res_in[0:M, r, :], ALPHA,
                                                 ps_s[0:M, bank:bank + 2, :].rearrange("p a b -> p (a b)"),
                                                 ALU.mult, ALU.add).then_inc(S["y_free"], 1)
                        dve.wait_ge(S["y_free"], it["upto"]["yy"])
                    for j in range(2):
                        st = dve.bn_stats(stats[0:M, r, 6 * j:6 * j + 6], z[:, 512 * j:512 * (j + 1)])
                    link(st)
                    dve.bn_aggr(mv[0:M, r, :], stats[0:M, r, :]).then_inc(S["ln_var"], 1)
                    dve.wait_ge(S["ln_rs"], ln + 1)
                    if ln >= 2:
                        dve.wait_ge(x_st[r], 16 * (ln // 2))
                        if it["xprev"]:
                            dve.wait_ge(S["t_full"], it["xprev"])
                    xn = x_new[0:M, r, :]
                    link(dve.tensor_scalar(xn, z, mv[0:M, r, 0:1], rstd[0:M, r, 0:1], ALU.subtract, ALU.mult))
                    link(dve.tensor_tensor(xn, xn, ln_g[0:M, :], ALU.mult))
                    dve.tensor_tensor(xn, xn, ln_b[0:M, :], ALU.add).then_inc(S["ln_done"], 1)
                elif kind == "cum":
                    dve.wait_ge(S["pj_act"], it["upto"]["pj_act"])
                    dve.tensor_scalar(iws, fz[:, :, NH:2 * NH], IW_SCALE, None, ALU.mult)
                    link(dve.tensor_tensor(f3[0], fz[:, :, 0:NH], bf[:, 72 * l:72 * (l + 1)]
                                           .rearrange("p (b h) -> p b h", b=NB), ALU.add))
                    link(dve.tensor_scalar(fw[:, 1, :], fw[:, 0, :], -1.0, None, ALU.mult))
                    dve.tensor_tensor(fw[:, 1, :], fw[:, 0, :], fw[:, 1, :], ALU.max).then_inc(S["fe_in"], 1)
                    dve.wait_ge(S["fe_out"], it["cum"] + 1)
                    e, s_, s2, acc = fw[:, 2, :], fw[:, 3, :], fw[:, 4, :], fw[:, 1, :]
                    link(dve.tensor_scalar(s_, e, 2.0, None, ALU.add))
                    link(dve.reciprocal(s_, s_))
                    link(dve.tensor_tensor(s_, s_, e, ALU.mult))
                    link(dve.tensor_tensor(s2, s_, s_, ALU.mult))
                    link(dve.tensor_scalar(acc, s2, 1.0 / 17, None, ALU.mult))
                    for d in (15, 13, 11, 9, 7, 5, 3):
                        link(dve.scalar_tensor_tensor(acc, acc, 1.0 / d, s2, ALU.add, ALU.mult))
                    link(dve.scalar_tensor_tensor(acc, acc, 1.0, s_, ALU.add, ALU.mult))
                    link(dve.tensor_scalar(fw[:, 0, :], fw[:, 0, :], 0.0, None, ALU.min))
                    link(dve.scalar_tensor_tensor(fw[:, 5, :], acc, -2.0, fw[:, 0, :], ALU.mult, ALU.add))
                    dve.tensor_scalar(f3[5][:, 0, :], f3[5][:, 0, :], rowmask, None, ALU.mult).then_inc(S["cum_in"], 1)
                elif kind == "ix":
                    i, n, ix = it["i"], it["n"], it["ix"]
                    sc = score[:, s_off[i]:s_off[i] + n]
                    w = iws[:, i, 2 * it["p"] + it["e"]:2 * it["p"] + it["e"] + 1]
                    src = probs[:, it["row"], PAD:PAD + n]
                    dve.wait_ge(S["relu_done"], ix + 1)
                    if it["first"]:
                        if i == 2:
                            for j in range(2):
                                dve.wait_ge(x_st[j], 16 * len([m for m in range(it["upto"]["ln"]) if m % 2 == j]))
                            dve.wait_ge(S["t_full"], it["upto"]["tg"])
                        dve.tensor_scalar(sc, src, w, None, ALU.mult).then_inc(S["acc_done"], 1)
                    else:
                        dve.wait_ge(S["acc_done"], ix - 6)
                        dve.scalar_tensor_tensor(sc, src, w, sc, ALU.mult, ALU.add).then_inc(S["acc_done"], 1)
                    if it["last"]:
                        dve.wait_ge(S["acc_done"], ix + 1)
                        link(dve.tensor_tensor(sc[:, n - BLK:n], sc[:, n - BLK:n], tri_b[:], ALU.add))
                        if i == NB - 1:
                            top["next"] = 0
                elif kind == "mt":
                    what = it["what"]
                    if what == "G":
                        for (g, bank, _, nth), (c0, w) in zip(it["groups"], it["chunks"]):
                            gcount[0] += 1
                            dve.wait_ge(S["gate_in"], gcount[0])
                            dve.scalar_tensor_tensor(gate[:, c0:c0 + w], gate[:, c0:c0 + w], 1.0,
                                                     ps_s[:, bank, 0:w], ALU.add, ALU.mult).then_inc(S["pj_dve"], 1)
                    if what == "KR":
                        for (g, bank, _, nth), (c0, w) in zip(it["groups"], CHUNKS):
                            dve.wait_ge(S["pj_full"], g + 1)
                            cs = slice(c0, c0 + w)
                            dve.tensor_tensor(rtmp[64:96, 0:w], ps_s[96:128, bank, 0:w], rope_t[96:128, cs], ALU.mult)
                            link(dve.tensor_tensor(k_t[0][64:96, cs], ps_s[64:96, bank, 0:w], rope_t[64:96, cs], ALU.mult))
                            link(dve.tensor_tensor(k_t[0][64:96, cs], k_t[0][64:96, cs], rtmp[64:96, 0:w], ALU.add))
                            dve.tensor_copy(k_t[1][64:96, cs], k_t[0][64:96, cs]).then_inc(S["pj_dve"], 1)
                    top_ops(l, 2 * len(it["chunks"]))
                elif kind == "qb":
                    for (g, bank, _, nth), (c0, w) in zip(it["groups"], CHUNKS):
                        hcount[0] += 1
                        dve.wait_ge(S["half_done"], hcount[0])
                        q = q_t[it["h"] % 2][64:96, c0:c0 + w]
                        dve.scalar_tensor_tensor(rtmp[64:96, 0:w], ps_s[96:128, bank, 0:w], B_SCALE,
                                                 rope_t[96:128, c0:c0 + w], ALU.mult, ALU.mult)
                        link(dve.scalar_tensor_tensor(q, ps_s[64:96, bank, 0:w], B_SCALE,
                                                      rope_t[64:96, c0:c0 + w], ALU.mult, ALU.mult))
                        dve.tensor_tensor(q, q, rtmp[64:96, 0:w], ALU.add).then_inc(S["pj_dve"], 1)
                        dve.wait_ge(S["pj_dve"], nth)
                elif kind == "ct":
                    c = it["cn"]
                    dve.wait_ge(S["cn_rs"], c + 1)
                    dve.tensor_scalar(cn[:, c % 2, 0:Q_RANK], cn[:, c % 2, 0:Q_RANK], crs[:, c % 2, 0:1], None, ALU.mult)
                    dve.tensor_scalar(cn[:, c % 2, Q_RANK:384], cn[:, c % 2, Q_RANK:384], crs[:, c % 2, 1:2], None,
                                      ALU.mult).then_inc(S["cn_done"], 1)
                elif kind == "qk":
                    br, step = it["br"], it["step"]
                    M = ln_rows(it["i"])
                    if br == "C" and it["h"] == 0 and it["i"] == NB - 1:
                        top_ops(l, TOP_OPS)
                    dve.wait_ge(S["s_full"], step + 1)
                    nm = nmax[0:M, step % 4:step % 4 + 1]
                    m = dve.tensor_reduce(nm, ps_s[0:M, it["bank"]:it["bank"] + it["nb"], 0:it["w"]], AX.XY,
                                          ALU.max, negate=True)
                    if br == "D":
                        link(m)
                        s0 = NH * l + it["h"]
                        m = dve.tensor_tensor(nm, nm, nsink[0:M, s0:s0 + 1], ALU.min)
                    m.then_inc(S["max_done"], 1)
                    if br != "C":
                        top_ops(l, 1)
                elif kind == "rec":
                    step = it["step"]
                    M = ln_rows(it["i"])
                    c = slice(step % 4, step % 4 + 1)
                    dve.wait_ge(S["exp_done"], step + 1)
                    if it["br"] == "D":
                        dve.wait_ge(S["es_done"], it["ds"] + 1)
                        link(dve.tensor_tensor(psums[0:M, c], psums[0:M, c], esink[0:M, c], ALU.add))
                    link(dve.reciprocal(rinv[0:M, c], psums[0:M, c]))
                    off = p_off(it["br"], it["i"])
                    p = probs[0:M, it["row"], off:off + it["n"]]
                    dve.tensor_scalar(p, p, rinv[0:M, c], None, ALU.mult).then_inc(S["nrm_done"], 1)
                    top_ops(l, 1)
                elif kind == "pv":
                    og, a = it["og"], it["a"]
                    r0 = HD * (it["h"] % 2)
                    c0, w = (0, N_META) if a == 0 else (N_META + 256 * (a - 1), 256)
                    dve.wait_ge(S["pv_done"], og + 1)
                    if og >= 4:
                        dve.wait_ge(mx_st[og % 4], 16 * (og // 4))
                    dve.wait_ge(S["pj_dve"], gate_ready[og])
                    dve.scalar_tensor_tensor(mixg[r0:r0 + HD, og % 4, 0:w], ps_o[r0:r0 + HD, og % 2, 0:w], 0.5,
                                             gate[r0:r0 + HD, c0:c0 + w], ALU.mult, ALU.mult).then_inc(S["o_free"], 1)

        @block.gpsimd
        def _(pool):
            chain = [0]

            def link(ins):
                chain[0] += 1
                ins.then_inc(S["pool_chain"], 1)
                pool.wait_ge(S["pool_chain"], chain[0])

            nc.gpsimd.memset(xT[:, :, 0:PAD], 0.0).then_inc(S["zero_done"], 1)
            pool.wait_ge(S["consts"], 16 * 9)
            pool.wait_ge(S["zero_done"], 1)
            for it in items:
                kind, l = it["kind"], it["l"]
                if kind == "ln":
                    M, r = ln_rows(it["b"]), it["ln"] % 2
                    pool.wait_ge(S["ln_var"], it["ln"] + 1)
                    link(nc.gpsimd.tensor_scalar(rstd[0:M, r, 1:2], mv[0:M, r, 1:2], LN_EPS, None, ALU.add))
                    nc.gpsimd.tensor_tensor(rstd[0:M, r, 0:1], rstd[0:M, r, 1:2], halfneg[0:M, :],
                                            ALU.pow).then_inc(S["ln_rs"], 1)
                    pool.wait_ge(S["ln_rs"], it["ln"] + 1)
                elif kind == "tm" and it["what"] == "TB":
                    r = it["cn"] % 2
                    pool.wait_ge(S["pj_act"], it["groups"][0][3])
                    if it["cn"] >= 2:
                        pool.wait_ge(S["cn_done"], it["cn"] - 1)
                    link(nc.gpsimd.tensor_scalar(crs[:, r, 0:1], cstat[:, r, 0:1], 1.0 / Q_RANK, RMS_EPS,
                                                 ALU.mult, ALU.add))
                    link(nc.gpsimd.tensor_scalar(crs[:, r, 1:2], cstat[:, r, 1:2], 1.0 / KV_RANK, RMS_EPS,
                                                 ALU.mult, ALU.add))
                    link(nc.gpsimd.tensor_tensor(crs[:, r, 0:1], crs[:, r, 0:1], halfneg, ALU.pow))
                    nc.gpsimd.tensor_tensor(crs[:, r, 1:2], crs[:, r, 1:2], halfneg, ALU.pow).then_inc(S["cn_rs"], 1)
                    pool.wait_ge(S["cn_rs"], it["cn"] + 1)
                elif kind == "ms":
                    what = it["what"]
                    if what == "start":
                        if l > 0:
                            pool.wait_ge(S["y_full"], it["upto"]["yy"])
                        link(nc.gpsimd.memset(k_t[0][HD:BLK, :], 0.0))
                        nc.gpsimd.memset(k_t[1][0:HD, :], 0.0).then_inc(S["ms_done"], 1)
                    elif what == "A":
                        pool.wait_ge(S["relu_full"], it["upto"]["ix"])
                        pool.wait_ge(S["cum_stored"], 32 * (l + 1))
                        link(nc.gpsimd.memset(probs[:, :, 0:PAD], 0.0))
                        link(nc.gpsimd.memset(probs_t[:, :, 8, 0:BLK], 0.0))
                        link(nc.gpsimd.memset(probs_t[:, :, 9, BLK:2 * BLK], 0.0))
                        link(nc.gpsimd.memset(q_t[0][HD:BLK, :], 0.0))
                        link(nc.gpsimd.memset(q_t[1][HD:BLK, :], 0.0))
                        link(nc.gpsimd.memset(k_t[1][HD:BLK, :], 0.0))
                        for t in (q_t[0], q_t[1], k_t[0], k_t[1]):
                            link(nc.gpsimd.memset(t[HD:HD + 2, :], 1.0))
                        nc.gpsimd.memset(small[:, 200:201], 0.0).then_inc(S["ms_done"], 1)
                    else:
                        pool.wait_ge(S["s_full"], it["upto"]["step"])
                        for t in (q_t[0], q_t[1], k_t[0], k_t[1]):
                            link(nc.gpsimd.memset(t[HD:BLK, :], 0.0))
                        nc.gpsimd.memset(small[:, 200:201], 0.0).then_inc(S["ms_done"], 1)
                    pool.wait_ge(S["ms_done"], it["ms"] + 1)


def p_off(br, i):
    return BLK * (i - 1) if br == "D" and i >= 2 else PAD


def runs(slots):
    out = []
    for c, s in enumerate(slots):
        if out and out[-1][1] + out[-1][2] == s:
            out[-1] = (out[-1][0], out[-1][1], out[-1][2] + 1)
        else:
            out.append((c, s, 1))
    return out


def feature_tiles():
    off, at = {}, 0
    for name, size in (("a_q", 512), ("a_k", 512), ("a_v", 512), ("a_f", 8), ("a_g", 512), ("b_cq", 256),
                       ("b_ckv", 128), ("b_kr", 32), ("b_g", 512), ("c_q", 512), ("c_k", 128), ("c_v", 128),
                       ("c_iq", 512), ("c_ik", 64), ("c_iw", 8), ("c_g", 512), ("d_q", 512), ("d_k", 128),
                       ("d_v", 128), ("d_g", 512)):
        off[name] = at
        at += size
    r = lambda name, a, n: list(range(off[name] + a, off[name] + a + n))
    kr = r("b_kr", 0, 32) + r("b_kr", 16, 16) + r("b_kr", 0, 16)
    tiles = []
    for it in Plan().items:
        if it["kind"] == "mt" and it["l"] == 0 and it["wt"] == len(tiles):
            w, p, h = it["what"], it.get("p"), it.get("h")
            br = it.get("br", "").lower()
            tiles.append({"IK": lambda: r("c_ik", 0, 64) * 2, "IQ": lambda: r("c_iq", 128 * p, 128),
                          "AQK": lambda: r("a_q", 64 * h, 64) + r("a_k", 64 * h, 64),
                          "G": lambda: r(br + "_g", 128 * p, 128), "K": lambda: r(br + "_k", 0, 128),
                          "Q": lambda: r(br + "_q", 128 * p, 128), "KR": lambda: kr * 2}[w]())
    rows = {"w_tc": r("c_v", 0, 128) + r("d_v", 0, 128) + r("a_f", 0, 8) + r("c_iw", 0, 8),
            "w_ta": r("a_v", 0, 512), "w_tb": r("b_cq", 0, 256) + r("b_ckv", 0, 128)}
    return tiles, rows


def kernel(**inputs):
    import numpy as np
    import concourse.bacc as bacc
    from concourse.bass_utils import run_bass_kernel_spmd

    a = {k: np.asarray(v) for k, v in inputs.items()}
    L = DEPTH

    def parts(w):
        return np.ascontiguousarray(w.reshape(L, -1, BLK, w.shape[-1]).transpose(0, 2, 1, 3)).reshape(L, BLK, -1)

    def spread(v):
        return np.ascontiguousarray(np.broadcast_to(v.reshape(1, -1), (BLK, v.size)))

    tiles, rows = feature_tiles()
    arrays = {"x": a["x"], "meta_tokens": a["meta_tokens"], "rel_bias": a["rel_bias"]}
    arrays["w_feat"] = np.stack([parts(a["w_in"][:, :, t]) for t in tiles], axis=1)
    for name, cols in rows.items():
        arrays[name] = parts(a["w_in"][:, :, cols])
    hq = [96 * h + c for h in range(NH) for c in list(range(96)) + list(range(80, 96)) + list(range(64, 80))]
    arrays["u_q"] = parts(a["w_uq"][:, :, hq])
    arrays["u_k"] = parts(a["w_ukv"][:, :, [128 * h + c for h in range(NH) for c in range(64)]])
    arrays["u_v"] = parts(a["w_ukv"][:, :, [128 * h + 64 + c for h in range(NH) for c in range(64)]])
    arrays["w_out"] = parts(a["w_out"]).reshape(L, BLK, 16, D_MODEL)
    arrays["ln_g"] = np.stack([spread(v) for v in (a["ln0_g"], *a["ln_g"])])
    arrays["ln_b"] = np.stack([spread(v) for v in (a["ln0_b"], *a["ln_b"])])
    arrays["b_f"] = spread(np.broadcast_to(a["b_f"][:, None, :], (L, NB, NH)))
    f32 = np.float32
    arrays["ident"] = np.eye(BLK, dtype=f32)
    arrays["anti"] = np.ascontiguousarray(np.eye(BLK, dtype=f32)[::-1])
    arrays["upper1"] = np.concatenate([np.triu(np.ones((BLK, BLK), f32)), np.ones((BLK, 3 * BLK), f32)], 1)
    small = np.zeros((BLK, 24), f32)
    small[PAD:, 0] = 1.0
    small[:, 1] = -0.5
    small[:, 2:6] = a["mla_gq"].reshape(2 * L, BLK).T
    small[:, 6:8] = a["mla_gkv"].T
    small[:, 8:24] = a["sinks"].reshape(1, -1)
    arrays["small"] = small
    half = ROPE // 2
    freqs = (f32(10000.0) ** (-np.arange(half, dtype=f32) / f32(half))).astype(f32)
    ang = freqs[:, None] * np.arange(NTOK, dtype=f32)[None, :]
    cos, sin = np.cos(ang).astype(f32), np.sin(ang).astype(f32)
    arrays["rope_t"] = np.concatenate([np.zeros((64, NTOK), f32), cos, cos, -sin, sin])
    dist = 255 - np.arange(LINE)
    n = np.maximum(dist, 0)
    large = 16 + (np.log(np.maximum(n, 1) / 16.0) / np.log(8.0) * 16 + 1e-9).astype(np.int64)
    bucket = np.where(n < 16, n, np.minimum(large, 31))
    hot = (np.arange(32)[:, None] == bucket[None, :]).astype(f32)
    near = hot.copy()
    near[31] -= 1.0
    near[:, dist < 0] = 0.0
    inside = (dist >= 0) & (dist < 128)
    arrays["onehot"] = np.concatenate([near, hot * inside], 1).astype(f32)
    arrays["lmask"] = np.ascontiguousarray(np.broadcast_to(
        np.concatenate([np.zeros(LINE), np.where(inside, 0.0, NEG)]).astype(f32), (NH, 2 * LINE)))

    nc = bacc.Bacc("TRN2", target_bir_lowering=False, num_devices=1)
    arrays = {"in_" + k: np.ascontiguousarray(v) for k, v in arrays.items()}
    t_in = {k[3:]: nc.dram_tensor(k, v.shape, mybir.dt.from_np(v.dtype), kind="ExternalInput").ap()
            for k, v in arrays.items()}
    out = nc.dram_tensor("out", (1, SEQ, D_MODEL), F32, kind="ExternalOutput").ap()
    build(nc, t_in, out)
    r = run_bass_kernel_spmd(nc, [arrays], core_ids=[0])
    return r.results[0]["out"]
```

```python
from contextlib import ExitStack

import concourse.bass as bass
from concourse import mybir

F32 = mybir.dt.float32
F32R = mybir.dt.float32r
BF16 = mybir.dt.bfloat16
ALU = mybir.AluOpType
ACT = mybir.ActivationFunctionType
AX = mybir.AxisListType

D_MODEL, SEQ, DEPTH = 1024, 1024, 2
N_META, BLK = 16, 128
PAD = BLK - N_META
NB = SEQ // BLK + 1
NPAD = NB * BLK
NTOK = NPAD - PAD
KT = D_MODEL // BLK
HD, NH = 64, 8
ROPE = 32
Q_RANK, KV_RANK = 256, 128
TOPK = 256
ALPHA = (2 * DEPTH) ** 0.25
LN_EPS, RMS_EPS = 1e-5, 1e-6
NEG = -1e30
TAKEN = -3e38
A_SCALE = HD ** -0.5
B_SCALE = (HD + ROPE) ** -0.5
IW_SCALE = NH ** -0.5
CHUNKS = [(0, 348), (348, 348), (696, 344)]
LAG = 2
ORDER = [8, 7, 0, 4, 3, 2, 1, 6, 5]
BANK = {8: 0, 7: 0, 0: 2, 4: 2, 3: 0, 2: 1, 1: 0, 6: 2, 5: 0}
MT_PER_LAYER = 40
LINE = 384
TOP_OPS = (NB - 2) * (TOPK // 4)


def keys_of(i):
    return N_META + BLK * i


def score_shape(br, i):
    n = keys_of(i)
    k0 = 0
    if br == "D" and i >= 2:
        k0, n = n - 2 * BLK, 2 * BLK
    nb = 1 if n <= 512 else (2 if n < 1024 else 4)
    if br == "D":
        bank = ORDER.index(i) % 3
    elif br == "I":
        bank = {8: 0, 7: 0, 6: 2, 5: 0, 4: 2, 3: 0, 2: 1}[i]
    else:
        bank = BANK[i]
    return k0, n, nb, n // nb, bank


def key_slots(br, i):
    if br == "D":
        return [(0, 0)] if i == 0 else ([(i - 1, 9), (i, 7)] if i % 2 else [(i - 1, 7), (i, 8)])
    return [(k, 8 if (k == i and i and i % 2 == 0) else k) for k in range(i + 1)]


def pair_slots(br, a):
    if a == 0:
        return [(0, 0)]
    if br == "D":
        return [(2 * a - 2, 9), (2 * a - 1, 7), (2 * a, 8)]
    return [(k, k) for k in range(2 * a)] + [(2 * a, 8)]


class Plan:

    def __init__(self):
        self.items = []
        self.n = dict(pj=0, step=0, ix=0, tg=0, og=0, wt=0, ln=0, cum=0, ms=0, yy=0, pu=0, cn=0, pv=0, ds=0, pj_act=0, pj_dve=0, hi=0)
        self.bank_owner = [None] * 4
        self.row_owner = [None] * 3
        self.hunit = 0
        self.ring = 0
        self.parts = {}
        self.xt_end = {}
        for b in range(NB):
            self.layer_norm(-1, b)
            if b == 1:
                self.add("start", l=0)
            if b >= 2:
                self.token_block(0, "TC", b - 2)
            if b:
                self.x_transpose(-1, b - 1)
        self.token_block(0, "TC", NB - 2)
        self.x_transpose(-1, NB - 1)
        self.token_block(0, "TC", NB - 1)
        for l in range(DEPTH):
            self.layer(l)

    def add(self, kind, **kw):
        kw["kind"] = kind
        kw["upto"] = dict(self.n)
        self.items.append(kw)
        return kw

    def take(self, key, k=1):
        v = self.n[key]
        self.n[key] += k
        return v

    def banks(self, which, event):
        old = [self.bank_owner[b] for b in which if self.bank_owner[b]]
        for b in which:
            self.bank_owner[b] = event
        return latest(old)

    def row(self, event):
        r = self.take("pu") % 3
        old = self.row_owner[r]
        self.row_owner[r] = event
        return r, latest([old] if old else [])

    def pj_groups(self, count, by="act", bank=None):
        out = []
        for _ in range(count):
            g, k = self.take("pj"), self.take("pj_" + by)
            c = bank
            if bank is None:
                c = self.ring
                self.ring = (self.ring + 1) % 4
            out.append((g, c, self.banks([c], ("pj_" + by, k + 1)), k + 1))
        return out

    def mt(self, l, what, **kw):
        self.part(l, self.take("wt"), what, [0, 1, 2], **kw)

    def part(self, l, wt, what, chunks, bank=None, **kw):
        self.parts[wt] = self.parts.get(wt, 0) + len(chunks)
        self.add("mt", l=l, what=what, wt=wt, chunks=[CHUNKS[c] for c in chunks], last=self.parts[wt] == 3,
                 groups=self.pj_groups(len(chunks), "dve", bank),
                 hi=self.take("hi", len(chunks)) if what not in ("G", "KR") else None, **kw)

    def token_block(self, l, what, b):
        self.add("tm", l=l, what=what, b=b, groups=self.pj_groups(1), cn=NB * l + b)

    def tm(self, l, what):
        for b in range(NB):
            self.token_block(l, what, b)
            if what == "TB" and b:
                self.add("ct", l=l, b=b - 1, cn=NB * l + b - 1, tg=self.take("tg"))
        if what == "TB":
            self.add("ct", l=l, b=NB - 1, cn=NB * l + NB - 1, tg=self.take("tg"))

    def ms(self, l, what):
        self.add("ms", l=l, what=what, ms=self.take("ms"))

    def layer_norm(self, l, b):
        ln = self.take("ln")
        self.add("ln", l=l, b=b, ln=ln, xprev=self.xt_end.get(ln - 2))

    def x_transpose(self, l, b):
        ln = (l + 1) * NB + b
        tg = self.take("tg", 2)
        self.xt_end[ln] = tg + 2
        self.add("xt", l=l, b=b, ln=ln, tg=tg)

    def layer(self, l):
        if l:
            self.add("start", l=l)
            self.tm(l, "TC")
        cum = self.take("cum")
        self.add("cum", l=l, cum=cum, waits=self.banks([0, 1, 2], ("cum_free", cum + 1)))
        self.mt(l, "IK")
        self.mt(l, "IQ", p=0)
        for p in range(4):
            for e in range(2):
                for i in range(2, NB):
                    ix = self.take("ix")
                    k0, n, nb, w, bank = score_shape("I", i)
                    waits = self.banks(range(bank, bank + nb), ("relu_done", ix + 1))
                    row, rwaits = self.row(("acc_done", ix + 1))
                    self.add("ix", l=l, p=p, e=e, i=i, ix=ix, n=n, nb=nb, w=w, bank=bank, waits=waits,
                             row=row, rwaits=rwaits, first=(p == 0 and e == 0), last=(p == 3 and e == 1))
                    if e == 1 and i == 4 and p < 3:
                        self.mt(l, "IQ", p=p + 1)
        self.tm(l, "TA")
        self.ms(l, "A")
        self.pending, self.pv_next, self.rec_next = [], None, None
        self.mt(l, "AQK", h=0)
        for h in range(NH):
            self.head(l, "A", h)
        self.mt(l, "K", br="D")
        for h in range(NH):
            if h == 0:
                self.mt(l, "Q", br="D", p=0)
            self.head(l, "D", h)
        self.flush()
        self.tm(l, "TB")
        self.add("uw", l=l)
        self.ms(l, "B")
        self.tm(l, "VB")
        self.mt(l, "KR")
        for h in range(NH):
            if h == 0:
                self.k_latent(l, 0, [0, 1, 2])
                self.q_latent(l, 0, [0, 1, 2])
            self.head(l, "B", h)
        self.mt(l, "K", br="C")
        for h in range(NH):
            if h == 0:
                self.mt(l, "Q", br="C", p=0)
            self.head(l, "C", h)
            if h == 0:
                self.add("w0", l=l)
        self.flush()
        self.add("wo", l=l)
        first = 0 if l < DEPTH - 1 else 1
        for b in range(first, NB):
            yy = self.take("yy")
            bank = 2 * (yy % 2)
            self.add("y", l=l, b=b, yy=yy, bank=bank, waits=self.banks([bank, bank + 1], ("y_free", yy + 1)),
                     first=(b == first))
            self.layer_norm(l, b)
            if l < DEPTH - 1 and b > first:
                self.x_transpose(l, b - 1)
        if l < DEPTH - 1:
            self.x_transpose(l, NB - 1)

    def lagged(self):
        s = self.pending.pop(0)
        self.values()
        self.add("tp", **s)
        if s["i"] % 2 or s["i"] == 0:
            self.pv_next = s

    def values(self):
        if self.pv_next:
            self.take("pv")
            self.add("pv", **self.pv_next)
            self.pv_next = None

    def normalise(self):
        if self.rec_next:
            self.add("rec", **self.rec_next)
            self.rec_next = None

    def flush(self):
        self.normalise()
        while self.pending:
            self.lagged()
        self.values()

    def head(self, l, br, h):
        hu = None
        if br in "CD":
            hu = self.hunit
            self.hunit += 1
        gate = nxt = None
        if h % 2 == 0:
            wt = self.take("wt")
            gate = lambda c, bank: self.part(l, wt, "G", [c], bank=bank, br=br, p=h // 2)
        if br == "A" and h + 1 < NH:
            wn = self.take("wt")
            nxt = lambda c, bank: self.part(l, wn, "AQK", [c], bank=bank, h=h + 1)
        if br == "B" and h + 1 < NH:
            nxt = lambda c, bank: self.q_latent(l, h + 1, [c], bank)
        if br in "CD" and h % 2 and h + 1 < NH:
            wq = self.take("wt")
            pair = lambda c, bank: self.part(l, wq, "Q", [c], bank=bank, br=br, p=(h + 1) // 2)
        elif br == "B" and h % 2 and h + 1 < NH:
            pair = lambda c, bank: self.k_latent(l, (h + 1) // 2, [c], bank)
        else:
            pair = None
        fill, last = {}, []
        if gate:
            fill[0], fill[4], fill[6] = [(gate, 0, 3)], [(gate, 2, 1)], [(gate, 1, 1)]
            if nxt:
                fill[1] = [(nxt, 0, 1)]
                fill[5] = [(nxt, 1, 2), (nxt, 2, 3)]
        elif nxt:
            fill[0], fill[4], fill[6] = [(nxt, 0, 3)], [(nxt, 1, 1)], [(nxt, 2, 1)]
        if pair:
            fill[5] = [(pair, 0, 3), (pair, 1, 2 if br != "D" else 3)]
            last = [(pair, 2, 3)]
        for i in ORDER:
            step = self.take("step")
            k0, n, nb, w, bank = score_shape(br, i)
            waits = self.banks(range(bank, bank + nb), ("exp_done", step + 1))
            slots = key_slots(br, i)
            ntg = -(-len(slots) // 4)
            tg = self.take("tg", ntg)
            row, rwaits = self.row(("t_full", tg + ntg))
            a = (i + 1) // 2
            og = self.n["og"]
            if i % 2 or i == 0:
                self.take("og")
            s = dict(l=l, br=br, h=h, i=i, step=step, k0=k0, n=n, nb=nb, w=w, bank=bank, waits=waits,
                     slots=slots, tg=tg, ntg=ntg, row=row, rwaits=rwaits, a=a, og=og, hu=hu,
                     ds=self.take("ds") if br == "D" else None)
            self.normalise()
            self.add("qk", **s)
            self.rec_next = s
            self.pending.append(s)
            if i in fill:
                for piece, c, b in fill[i]:
                    piece(c, 3 if br == "D" else b)
            if len(self.pending) > LAG:
                self.lagged()
        for piece, c, bank in last:
            piece(c, bank)
        self.ring = 2

    def k_latent(self, l, p, chunks, bank=None):
        self.add("kb", l=l, p=p, chunks=[CHUNKS[c] for c in chunks], groups=self.pj_groups(len(chunks), "act", bank))

    def q_latent(self, l, h, chunks, bank=None):
        self.add("qb", l=l, h=h, chunks=[CHUNKS[c] for c in chunks],
                 groups=self.pj_groups(len(chunks), "dve", bank))


def latest(events):
    out = {}
    for name, v in events:
        out[name] = max(out.get(name, 0), v)
    return sorted(out.items())


def build(nc, t_in, out):
    plan = Plan()
    items = plan.items
    resid = [nc.dram_tensor(f"resid{l}", (NTOK, D_MODEL), F32, kind="Internal").ap() for l in range(DEPTH)]
    mixed = [nc.dram_tensor(f"mixed{l}", (16, BLK, NTOK), F32, kind="Internal").ap() for l in range(DEPTH)]
    lines = nc.dram_tensor("lines", (2 * NH, LINE), F32, kind="Internal")

    ctx = ExitStack()
    with ctx:
        def sb(name, shape, dt=F32):
            return ctx.enter_context(nc.sbuf_tensor(name, shape, dt))

        def sem(name):
            return ctx.enter_context(nc.semaphore(name))

        nV, nVC, nPT, nP, nW = NB * 512, NB * 256, 2 * 10 * 256, 3 * NPAD, 2 * KT * BLK
        arena = sb("arena", [BLK, nV + nVC + nPT + nP + nW])
        o = 0
        v_tok = arena[:, o:o + nV].rearrange("p (b c) -> p b c", b=NB); o += nV
        vc_tok = arena[:, o:o + nVC].rearrange("p (b c) -> p b c", b=NB); o += nVC
        probs_t = arena[:, o:o + nPT].rearrange("p (g s q) -> p g s q", g=2, s=10); o += nPT
        probs = arena[:, o:o + nP].rearrange("p (r k) -> p r k", r=3); o += nP
        w_ring = arena[:, o:o + nW].rearrange("p (s k c) -> p s k c", s=2, k=KT); o += nW
        w_first = arena[:, nV + nVC:nV + nVC + KT * 272]
        w_out = arena[:, 0:16 * D_MODEL].rearrange("p (k n) -> p k n", k=16)
        with nc.sbuf_tensor("qk", [BLK, 4 * NTOK], F32) as qk:
            pass
        q_t = [qk[:, e * NTOK:(e + 1) * NTOK] for e in range(2)]
        k_t = [qk[:, (2 + e) * NTOK:(3 + e) * NTOK] for e in range(2)]
        parts = sb("parts", [BLK, 6, NTOK], F32R)
        qs, k_hi, k_lo = parts[:, 0:2], parts[:, 2:4], parts[:, 4:6]
        mix_in = qk[:, 0:4096].rearrange("p (r k t) -> p r k t", r=2, k=16)
        vw = sb("vw", [BLK, KT * 512])
        u_q = vw[:, 0:2048].rearrange("p (k c) -> p k c", k=2)
        u_k = vw[:, 2048:2560]
        u_v = vw[:, 2560:3072]
        ln_g, ln_b = vw[:, 0:1024], vw[:, 1024:2048]
        z_sum = vw[:, 2048:4096].rearrange("p (r n) -> p r n", r=2)
        s_off = {}
        so = 0
        for i in range(2, NB):
            s_off[i] = so
            so += keys_of(i)
        score = sb("score", [BLK, so])
        res_in = score[:, 0:2048].rearrange("p (r n) -> p r n", r=2)
        x_new = score[:, 2048:4096].rearrange("p (r n) -> p r n", r=2)
        xT = sb("xT", [BLK, KT, NPAD])
        with nc.sbuf_tensor("cT", [BLK, 3, NPAD], F32) as cT:
            pass
        fox = sb("fox", [BLK, 3, NPAD], F32R)
        head_rows = fox[:, 1, 0:NH * BLK]
        decay = fox[:, 2]
        sel = sb("sel", [BLK, so], BF16)
        gate = sb("gate", [BLK, NTOK])
        mixg = sb("mixg", [BLK, 2, 256])
        hankel = sb("hankel", [BLK, 256])
        bias = sb("bias", [BLK, 2, 2, 256], F32R)
        rope_t = sb("rope_t", [BLK, NTOK])
        cn = gate[:, 0:2 * (Q_RANK + KV_RANK)].rearrange("p (r c) -> p r c", r=2)
        ident = sb("ident", [BLK, BLK])
        anti = sb("anti", [BLK, BLK], F32R)
        ident_b = sb("ident_b", [BLK, BLK], BF16)
        tri_b = sb("tri_b", [BLK, BLK], BF16)
        upper1 = mixg[:, 0:2, :].rearrange("p g q -> p (g q)")
        rel = sb("rel", [32, 2 * NH])
        onehot = cT[0:32, 1, 0:2 * LINE]
        lmask = cT[0:NH, 0, 0:2 * LINE]
        line_sb = cT[0:NH, 2, 0:2 * LINE]
        small = sb("small", [BLK, 256])
        head_row = small[:, 240:248]
        rowmask = small[:, 0:1]
        halfneg = small[:, 1:2]
        gq = small[:, 2:2 + 2 * DEPTH]
        gkv = small[:, 6:6 + DEPTH]
        sink = small[:, 8:8 + DEPTH * NH]
        nsink = small[:, 24:24 + DEPTH * NH]
        nmax = small[:, 40:44]
        psums = small[:, 44:48]
        rinv = small[:, 48:52]
        esink = small[:, 52:56]
        stats = small[:, 56:80].rearrange("p (r c) -> p r c", r=2)
        mv = small[:, 80:84].rearrange("p (r c) -> p r c", r=2)
        rstd = small[:, 84:88].rearrange("p (r c) -> p r c", r=2)
        top8 = small[:, 88:96]
        cstat = small[:, 96:100].rearrange("p (r c) -> p r c", r=2)
        crs = small[:, 100:104].rearrange("p (r c) -> p r c", r=2)
        iws = small[:, 104:176].rearrange("p (b h) -> p b h", b=NB)
        bf = sb("bf", [BLK, DEPTH * 72])
        fz = sb("fz", [BLK, NB, 16])
        fw = cT[:, 0, 0:6 * 72].rearrange("p (a b) -> p a b", a=6)
        f3 = [fw[:, j, :].rearrange("p (b h) -> p b h", b=NB) for j in range(6)]
        squares = sb("squares", [BLK, Q_RANK], BF16)

        ps_s = ctx.enter_context(nc.psum_tensor("ps_s", [BLK, 4, 512], F32))
        ps_t = ctx.enter_context(nc.psum_tensor("ps_t", [BLK, 2, 512], F32))
        ps_o = ctx.enter_context(nc.psum_tensor("ps_o", [BLK, 2, 512], F32))
        rtmp = sb("rtmp", [BLK, 348])
        anti_in = rtmp[:, 0:BLK]

        names = """pj_full pj_act pj_dve s_full relu_full relu_done acc_done max_done exp_done es_done 
                   nrm_done t_full pv_done o_free y_full y_free cum_in cum_full cum_free
                   ms_done mask_done ln_var ln_rs ln_done dve_chain pool_chain act_chain half_done gate_in
                   cn_raw cn_rs cn_done consts line_full line_ready line_stored lnp_ld fe_in fe_out top_step
                   zero_done small_done hi_done bias_done up_ld decay_hi decay_done""".split()
        S = {n: sem(n) for n in names}
        t_act, t_dve = sem("t_act"), sem("t_dve")
        w_ld = [sem(f"w_ld{i}") for i in range(2)]
        h_ld = sem("h_ld")
        mx_st = [sem(f"mx_st{i}") for i in range(2)]
        mb_ld = [sem(f"mb_ld{i}") for i in range(2)]
        r_ld = [sem(f"r_ld{i}") for i in range(2)]
        x_st = [sem(f"x_st{i}") for i in range(2)]
        vw_ld = sem("vw_ld")
        wo_ld = [sem(f"wo_ld{i}") for i in range(4)]
        block = ctx.enter_context(nc.Block())

        def vw_need(l, what):
            return 16 * (6 * l + {"TC": 1, "TA": 2, "TB": 3, "VB": 6}[what])

        w_used, vw_used, head_end, head_of = {}, {}, {}, {}
        for it in items:
            if it["kind"] == "mt":
                w_used[it["wt"]] = it["groups"][-1][0] + 1
            if it["kind"] == "tm":
                vw_used[(it["l"], it["what"])] = it["groups"][-1][0] + 1
            if it["kind"] == "qb":
                vw_used[(it["l"], "U")] = it["groups"][-1][0] + 1
            if it["kind"] == "qk":
                if it["hu"] is not None:
                    head_end[it["hu"]] = it["step"] + 1
                    head_of[it["hu"]] = (it["l"], it["br"], it["h"])

        ct_end = {it["cn"]: it["tg"] + 1 for it in items if it["kind"] == "ct"}
        c_end = {it["l"]: it["step"] + 1 for it in items if it["kind"] == "qk" and it["br"] == "C"}
        gate_ready, at = {}, 0
        for it in items:
            if it["kind"] == "mt" and it["what"] == "G":
                at = it["groups"][-1][3]
            if it["kind"] == "pv":
                gate_ready[it["og"]] = at
        gcount, hcount = [0], [0]
        f_tmp = cT[:, 0, 1024:1152]

        by_act = []
        for it in items:
            if it["kind"] in ("xt", "ct", "tp"):
                for tg in range(it["tg"], it["tg"] + {"xt": 2, "ct": 1}.get(it["kind"], it.get("ntg"))):
                    by_act.append((tg, tg % 2 == 0 or it.get("br") in ("A", "D")))
        by_act = [v for _, v in sorted(by_act)]

        def all_left(eng, n):
            if n:
                act_n = sum(by_act[:n])
                if act_n:
                    eng.wait_ge(t_act, act_n)
                if n - act_n:
                    eng.wait_ge(t_dve, n - act_n)

        def bank_left(eng, tg):
            if tg >= 2:
                n = sum(by_act[:tg - 1])
                if by_act[tg - 2]:
                    eng.wait_ge(t_act, n)
                else:
                    eng.wait_ge(t_dve, tg - 1 - n)

        def ln_rows(b):
            return N_META if b == 0 else BLK

        def tok0(b):
            return 0 if b == 0 else N_META + BLK * (b - 1)

        def col0(b):
            return PAD if b == 0 else BLK * b

        def waits(eng, pairs):
            for name, v in pairs:
                eng.wait_ge(S[name], v)

        def k_index(br, h):
            return h % 2 if br in "AB" else h // (NH // 2)

        def lnset(l):
            return l + 1

        @block.sync
        def _(sp):
            for dst, src in ((ident, "ident"), (anti_in, "anti"), (upper1, "upper1"), (rel, "rel_bias"),
                             (rope_t, "rope_t"), (bf, "b_f")):
                sp.dma_start(dst[:], t_in[src]).then_inc(S["consts"], 16)
            sp.dma_start(onehot, t_in["onehot"]).then_inc(S["consts"], 16)
            sp.dma_start(lmask, t_in["lmask"]).then_inc(S["consts"], 16)
            sp.dma_start(small[:, 0:24], t_in["small"]).then_inc(S["consts"], 16)
            sp.dma_start(head_row, t_in["head_row"]).then_inc(S["consts"], 16)

            def load_ln(l):
                sp.dma_start(ln_g, t_in["ln_g"][lnset(l)]).then_inc(S["lnp_ld"], 16)
                sp.dma_start(ln_b, t_in["ln_b"][lnset(l)]).then_inc(S["lnp_ld"], 16)

            def load_w_out(l, j):
                sp.dma_start(w_out[:, 4 * j:4 * j + 4, :], t_in["w_out"][l, :, 4 * j:4 * j + 4, :]
                             ).then_inc(wo_ld[j], 16)

            def store_lines():
                sp.wait_ge(S["line_ready"], 1)
                for j in range(2):
                    sp.dma_start(lines.ap()[NH * j:NH * (j + 1), :], line_sb[:, LINE * j:LINE * (j + 1)]
                                 ).then_inc(S["line_stored"], 16)

            def load_w(wt):
                if wt >= DEPTH * MT_PER_LAYER:
                    return
                if wt >= 2:
                    sp.wait_ge(S["pj_full"], w_used[wt - 2])
                sp.dma_start(w_ring[:, wt % 2], t_in["w_feat"][wt // MT_PER_LAYER, wt % MT_PER_LAYER]
                             ).then_inc(w_ld[wt % 2], 16)

            def load_hankel(hu):
                if hu >= 2 * DEPTH * NH:
                    return
                if hu:
                    sp.wait_ge(S["bias_done"], hu)
                l, br, h = head_of[hu]
                src = bass.AP(lines, ((0 if br == "C" else NH) + h) * LINE, [[1, BLK], [1, 256]])
                sp.dma_start(hankel[:], src).then_inc(h_ld, 16)

            load_ln(-1)
            x_dram = t_in["x"]
            for it in items:
                kind, l = it["kind"], it["l"]
                if kind == "ln":
                    ln, b = it["ln"], it["b"]
                    M = ln_rows(b)
                    if l < 0:
                        if ln >= 2:
                            sp.wait_ge(S["ln_done"], ln - 1)
                        src = t_in["meta_tokens"] if b == 0 else x_dram[0, BLK * (b - 1):BLK * b, :]
                        sp.dma_start(res_in[0:M, ln % 2, :], src).then_inc(r_ld[ln % 2], 16)
                    done = [(ln - 1, b - 1)] if b > (1 if l == DEPTH - 1 else 0) else []
                    if b == NB - 1:
                        done.append((ln, b))
                    for n, c in done:
                        sp.wait_ge(S["ln_done"], n + 1)
                        M = ln_rows(c)
                        dst = resid[l + 1][tok0(c):tok0(c) + M, :] if l < DEPTH - 1 else out[0, BLK * (c - 1):BLK * c, :]
                        sp.dma_start(dst, x_new[0:M, n % 2, :]).then_inc(x_st[n % 2], 16)
                if kind == "start":
                    if l == 0:
                        sp.dma_start(w_first, t_in["w_tc"][l]).then_inc(vw_ld, 16)
                    else:
                        sp.wait_ge(S["ln_done"], it["upto"]["ln"])
                        sp.wait_ge(S["y_free"], it["upto"]["yy"])
                        sp.dma_start(vw[:, 0:KT * 272], t_in["w_tc"][l]).then_inc(vw_ld, 16)
                        sp.wait_ge(S["y_full"], it["upto"]["yy"])
                        sp.dma_start(upper1, t_in["upper1"]).then_inc(S["up_ld"], 16)
                    for j in range(2):
                        wt = it["upto"]["wt"] + j
                        sp.dma_start(w_ring[:, wt % 2], t_in["w_feat"][l, j]).then_inc(w_ld[wt % 2], 16)
                    if l == 0:
                        store_lines()
                if kind == "cum":
                    sp.wait_ge(S["pj_full"], vw_used[(l, "TC")])
                    sp.dma_start(vw[:, 0:KT * 512], t_in["w_ta"][l]).then_inc(vw_ld, 16)
                if kind == "ms" and it["what"] == "A":
                    sp.wait_ge(S["ms_done"], it["ms"] + 1)
                    sp.wait_ge(S["pj_full"], vw_used[(l, "TA")])
                    sp.dma_start(vw[:, 0:KT * 384], t_in["w_tb"][l]).then_inc(vw_ld, 16)
                    if l == 0:
                        sp.wait_ge(S["line_stored"], 32)
                        load_hankel(0)
                if kind == "mt" and it["last"] and (it["wt"] % MT_PER_LAYER) < MT_PER_LAYER - 2:
                    load_w(it["wt"] + 2)
                if kind == "uw":
                    sp.wait_ge(S["pj_full"], vw_used[(l, "TB")])
                    sp.dma_start(vw[:, 0:2048], t_in["u_q"][l]).then_inc(vw_ld, 16)
                    sp.dma_start(u_k, t_in["u_k"][l]).then_inc(vw_ld, 16)
                    sp.dma_start(u_v, t_in["u_v"][l]).then_inc(vw_ld, 16)
                if kind == "pv":
                    og, a = it["og"], it["a"]
                    r0 = HD * (it["h"] % 2)
                    c0, w = (0, N_META) if a == 0 else (N_META + 256 * (a - 1), 256)
                    tile = "ABCD".index(it["br"]) * 4 + it["h"] // 2
                    sp.wait_ge(S["o_free"], og + 1)
                    sp.dma_start(mixed[l][tile, r0:r0 + HD, c0:c0 + w], mixg[r0:r0 + HD, og % 2, 0:w]
                                 ).then_inc(mx_st[og % 2], 16)
                if kind == "qk" and it["hu"] is not None and it["i"] == NB - 1:
                    load_hankel(it["hu"] + 1)
                if kind == "w0":
                    sp.wait_ge(S["pv_done"], it["upto"]["pv"])
                    load_w_out(l, 0)
                if kind == "wo":
                    sp.wait_ge(S["pv_done"], it["upto"]["pv"])
                    load_ln(l)
                    for j in range(2):
                        sp.wait_ge(mx_st[j], 16 * len([g for g in range(it["upto"]["og"]) if g % 2 == j]))
                    for j in range(2):
                        sp.wait_ge(x_st[j], 16 * len([n for n in range(it["upto"]["ln"]) if n % 2 == j]))
                if kind == "y":
                    yy, b, ln = it["yy"], it["b"], it["upto"]["ln"]
                    M = ln_rows(b)
                    if yy >= 2:
                        sp.wait_ge(S["y_full"], yy - 1)
                    sp.wait_ge(S["ln_done"], ln - 1)
                    sp.dma_start(mix_in[:, yy % 2, :, 0:M], mixed[l][:, :, tok0(b):tok0(b) + M]
                                 .rearrange("k p t -> p k t")).then_inc(mb_ld[yy % 2], 16)
                    sp.dma_start(res_in[0:M, ln % 2, :], resid[l][tok0(b):tok0(b) + M, :]).then_inc(r_ld[ln % 2], 16)
                    if it["first"]:
                        for j in range(1, 4):
                            load_w_out(l, j)
            for j in range(2):
                sp.wait_ge(x_st[j], 16 * len([n for n in range(plan.n["ln"]) if n % 2 == j]))

        @block.tensor
        def _(pe):
            pe.wait_ge(S["consts"], 16 * 10)
            pe.wait_ge(S["small_done"], 1)
            pe.matmul(ps_o[0:NH, 0, 0:LINE], rel[:, 0:NH], onehot[:, 0:LINE], start=True, stop=True)
            pe.matmul(ps_o[0:NH, 1, 0:LINE], rel[:, NH:2 * NH], onehot[:, LINE:2 * LINE],
                      start=True, stop=True).then_inc(S["line_full"], 1)
            for it in items:
                kind, l = it["kind"], it["l"]
                if kind == "xt":
                    M = ln_rows(it["b"])
                    pe.wait_ge(S["ln_done"], it["ln"] + 1)
                    for j in range(2):
                        tg = it["tg"] + j
                        bank_left(pe, tg)
                        for c in range(4):
                            k = 4 * j + c
                            mm = pe.transpose(ps_t[:, tg % 2, c * BLK:c * BLK + M],
                                              x_new[0:M, it["ln"] % 2, k * BLK:(k + 1) * BLK], ident[0:M, 0:M])
                        mm.then_inc(S["t_full"], 1)
                elif kind == "tm":
                    b, what = it["b"], it["what"]
                    g, bank, free, _ = it["groups"][0]
                    if b == 0:
                        pe.wait_ge(vw_ld, vw_need(l, what))
                    if b == 0 or (l == 0 and what == "TC"):
                        all_left(pe, it["upto"]["tg"])
                    waits(pe, free)
                    if what == "VB":
                        mm = pe.matmul(ps_s[:, bank, 0:512], cT[:, 2, b * BLK:(b + 1) * BLK], u_v,
                                       start=True, stop=True)
                    else:
                        n = {"TC": 272, "TA": 512, "TB": 384}[what]
                        wv = (w_first if l == 0 and what == "TC" else vw[:, 0:KT * n]).rearrange("p (k n) -> p k n", k=KT)
                        for k in range(KT):
                            mm = pe.matmul(ps_s[:, bank, 0:n], xT[:, k, b * BLK:(b + 1) * BLK], wv[:, k, :],
                                           start=(k == 0), stop=(k == KT - 1))
                    mm.then_inc(S["pj_full"], 1)
                elif kind == "ct":
                    tg = it["tg"]
                    pe.wait_ge(S["cn_done"], it["cn"] + 1)
                    bank_left(pe, tg)
                    for j in range(3):
                        mm = pe.transpose(ps_t[:, tg % 2, j * BLK:(j + 1) * BLK],
                                          cn[:, it["cn"] % 2, j * BLK:(j + 1) * BLK], ident[:])
                    mm.then_inc(S["t_full"], 1)
                elif kind == "cum":
                    pe.wait_ge(S["cum_in"], it["cum"] + 1)
                    if l > 0:
                        pe.wait_ge(S["up_ld"], 16 * l)
                    waits(pe, it["waits"])
                    for c in range(3):
                        for b in range(3 * c + 3):
                            j = max(b - 3 * c, 0)
                            src = upper1[:, 0:(3 - j) * BLK] if b >= 3 * c else upper1[:, BLK:4 * BLK]
                            mm = pe.matmul(ps_s[0:NH, c, j * BLK:3 * BLK], f3[5][:, b, :], src,
                                           start=(b == 0), stop=True, skip_group_check=(b > 0))
                    mm.then_inc(S["cum_full"], 1)
                elif kind == "mt":
                    wt = it["wt"]
                    pe.wait_ge(w_ld[wt % 2], 16 * (wt // 2 + 1))
                    for (g, bank, free, _), (c0, w) in zip(it["groups"], it["chunks"]):
                        waits(pe, free)
                        for k in range(KT):
                            mm = pe.matmul(ps_s[:, bank, 0:w], w_ring[:, wt % 2, k, :],
                                           xT[:, k, PAD + c0:PAD + c0 + w], start=(k == 0), stop=(k == KT - 1))
                        mm.then_inc(S["pj_full"], 1)
                elif kind == "qb":
                    for (g, bank, free, _), (c0, w) in zip(it["groups"], it["chunks"]):
                        waits(pe, free)
                        for k in range(2):
                            mm = pe.matmul(ps_s[:, bank, 0:w], u_q[:, k, it["h"] * BLK:(it["h"] + 1) * BLK],
                                           cT[:, k, PAD + c0:PAD + c0 + w], start=(k == 0), stop=(k == 1))
                        mm.then_inc(S["pj_full"], 1)
                elif kind == "kb":
                    for (g, bank, free, _), (c0, w) in zip(it["groups"], it["chunks"]):
                        waits(pe, free)
                        pe.matmul(ps_s[:, bank, 0:w], u_k[:, it["p"] * BLK:(it["p"] + 1) * BLK],
                                  cT[:, 2, PAD + c0:PAD + c0 + w], start=True, stop=True).then_inc(S["pj_full"], 1)
                elif kind == "ix":
                    i, w = it["i"], it["w"]
                    if i == 2:
                        waits(pe, [(n, it["upto"][n]) for n in ("pj_act", "pj_dve") if it["upto"][n]])
                    waits(pe, it["waits"])
                    q = parts[:, 4 * (it["p"] % 2) + it["e"], tok0(i):tok0(i) + BLK]
                    for c in range(it["nb"]):
                        for j in range(2):
                            mm = pe.matmul(ps_s[:, it["bank"] + c, 0:w], q, parts[:, 2 + j, c * w:(c + 1) * w],
                                           start=(j == 0), stop=(j == 1))
                    mm.then_inc(S["relu_full"], 1)
                elif kind == "qk":
                    br, h, i, w, nb = it["br"], it["h"], it["i"], it["w"], it["nb"]
                    M, r0 = (N_META, PAD) if i == 0 else (BLK, 0)
                    if i == NB - 1:
                        waits(pe, [(n, it["upto"][n]) for n in ("pj_act", "pj_dve") if it["upto"][n]])
                        pe.wait_ge(S["ms_done"], it["upto"]["ms"])
                        if br == "A":
                            pe.wait_ge(S["decay_done"], l + 1)
                        if it["hu"] is not None:
                            pe.wait_ge(S["bias_done"], it["hu"] + 1)
                    if br == "C" and h == 0 and i >= 2:
                        pe.wait_ge(S["mask_done"], 7 * l + (NB - i))
                    waits(pe, it["waits"])
                    j0 = k_index(br, h)
                    qc = slice(tok0(i), tok0(i) + M)
                    if br == "B":
                        terms = [(q_t[h % 2][:, qc], k_t[j0])]
                    else:
                        terms = [(qs[:, h % 2, qc], k_hi[:, j0]), (qs[:, h % 2, qc], k_lo[:, j0])]
                    if br == "A":
                        terms.append((head_rows[:, h * BLK:h * BLK + M], decay[:, PAD:NPAD]))
                    for c in range(nb):
                        dst = ps_s[0:M, it["bank"] + c, 0:w]
                        extra = []
                        if br == "C" and i >= 2:
                            m0 = s_off[i] + c * w
                            extra.append((dst, ident_b[:, r0:r0 + M], sel[:, m0:m0 + w]))
                        if c == nb - 1:
                            if br in "AB" or (br == "C" and i < 2):
                                extra.append((dst[:, w - min(w, M):w], ident_b[:, r0:r0 + M], tri_b[:, r0:BLK]))
                            if br in "CD":
                                wd = min(it["n"], 256)
                                for j in range(2):
                                    extra.append((dst[:, w - wd:w], anti[:, r0:r0 + M],
                                                  bias[:, it["hu"] % 2, j, 256 - wd:256]))
                        for j, (q, k) in enumerate(terms):
                            mm = pe.matmul(dst, q, k[:, it["k0"] + c * w:it["k0"] + (c + 1) * w],
                                           start=(j == 0), stop=(j == len(terms) - 1))
                        for j, (d2, lhs, rhs) in enumerate(extra):
                            mm = pe.matmul(d2, lhs, rhs, start=False, stop=True, skip_group_check=True)
                    mm.then_inc(S["s_full"], 1)
                elif kind == "tp":
                    M = ln_rows(it["i"])
                    pe.wait_ge(S["nrm_done"], it["step"] + 1)
                    for j in range(it["ntg"]):
                        tg = it["tg"] + j
                        bank_left(pe, tg)
                        for c, (kb, _) in enumerate(it["slots"][4 * j:4 * j + 4]):
                            mm = pe.transpose(ps_t[:, tg % 2, c * BLK:c * BLK + M],
                                              probs[0:M, it["row"], kb * BLK:(kb + 1) * BLK], ident[0:M, 0:M])
                        mm.then_inc(S["t_full"], 1)
                elif kind == "pv":
                    br, h, a, og = it["br"], it["h"], it["a"], it["og"]
                    all_left(pe, it["tg"] + it["ntg"])
                    if og >= 2:
                        pe.wait_ge(S["o_free"], og - 1)
                    w = N_META if a == 0 else 256
                    r0 = HD * (h % 2)
                    src = pair_slots(br, a)
                    for j, (kb, slot) in enumerate(src):
                        if br in "AB":
                            v = v_tok[:, kb, h * HD:(h + 1) * HD]
                        else:
                            c0 = (0 if br == "C" else 128) + HD * (h // (NH // 2))
                            v = vc_tok[:, kb, c0:c0 + HD]
                        mm = pe.matmul(ps_o[r0:r0 + HD, og % 2, 0:w], v, probs_t[:, og % 2, slot, 0:w],
                                       start=(j == 0), stop=(j == len(src) - 1))
                    mm.then_inc(S["pv_done"], 1)
                elif kind == "y":
                    yy, bank = it["yy"], it["bank"]
                    M = ln_rows(it["b"])
                    pe.wait_ge(mb_ld[yy % 2], 16 * (yy // 2 + 1))
                    waits(pe, it["waits"])
                    for k in range(16):
                        if it["first"] and k % 4 == 0:
                            pe.wait_ge(wo_ld[k // 4], 16 * (l + 1))
                        for half in range(2):
                            mm = pe.matmul(ps_s[0:M, bank + half, :], mix_in[:, yy % 2, k, 0:M],
                                           w_out[:, k, half * 512:(half + 1) * 512],
                                           start=(k == 0), stop=(k == 15))
                    mm.then_inc(S["y_full"], 1)


        @block.scalar
        def _(act):
            chain = [0]

            def link(ins):
                chain[0] += 1
                ins.then_inc(S["act_chain"], 1)
                act.wait_ge(S["act_chain"], chain[0])

            act.wait_ge(S["consts"], 16 * 10)
            order = list(items)
            for j in range(len(order) - 1):
                if order[j]["kind"] == "qk" and order[j + 1]["kind"] == "tp":
                    order[j], order[j + 1] = order[j + 1], order[j]
            for it in order:
                kind, l = it["kind"], it["l"]
                if kind == "xt":
                    b = it["b"]
                    M = ln_rows(b)
                    for tg in (it["tg"], it["tg"] + 1):
                        if by_act[tg]:
                            act.wait_ge(S["t_full"], tg + 1)
                            src = ps_t[:, tg % 2, :].rearrange("p (c t) -> p c t", c=4)[:, :, 0:M]
                            k = 4 * (tg - it["tg"])
                            nc.scalar.activation(xT[:, k:k + 4, col0(b):col0(b) + M], src, ACT.Copy).then_inc(t_act, 1)
                elif kind == "tm":
                    b, what = it["b"], it["what"]
                    g, bank, _, nth = it["groups"][0]
                    act.wait_ge(S["pj_full"], g + 1)
                    if what == "TB" and b == 0 and it["upto"]["pv"]:
                        act.wait_ge(S["o_free"], it["upto"]["pv"])
                    if what == "TC":
                        nc.scalar.activation(vc_tok[:, b, :], ps_s[:, bank, 0:256], ACT.Copy)
                        nc.scalar.activation(fz[:, b, :], ps_s[:, bank, 256:272], ACT.Copy).then_inc(S["pj_act"], 1)
                    elif what in ("TA", "VB"):
                        nc.scalar.activation(v_tok[:, b, :], ps_s[:, bank, :], ACT.Copy).then_inc(S["pj_act"], 1)
                    else:
                        c = it["cn"]
                        if c >= 2:
                            act.wait_ge(S["t_full"], ct_end[c - 2])
                        if b == 0:
                            act.wait_ge(S["line_stored"], 32)
                        nc.scalar.activation(cn[:, c % 2, :], ps_s[:, bank, 0:384], ACT.Copy)
                        link(nc.scalar.activation(squares[:, 0:Q_RANK], ps_s[:, bank, 0:Q_RANK], ACT.Square,
                                                  accum_out=cstat[:, c % 2, 0:1]))
                        nc.scalar.activation(squares[:, 0:KV_RANK], ps_s[:, bank, Q_RANK:384], ACT.Square,
                                             accum_out=cstat[:, c % 2, 1:2]).then_inc(S["pj_act"], 1)
                        act.wait_ge(S["pj_act"], nth)
                elif kind == "ct":
                    tg, b = it["tg"], it["b"]
                    if not by_act[tg]:
                        continue
                    act.wait_ge(S["t_full"], tg + 1)
                    for j in range(3):
                        gain = gq[:, 2 * l + j:2 * l + j + 1] if j < 2 else gkv[:, l:l + 1]
                        a = nc.scalar.activation(cT[:, j, b * BLK:(b + 1) * BLK], ps_t[:, tg % 2, j * BLK:(j + 1) * BLK],
                                                 ACT.Copy, scale=gain)
                    a.then_inc(t_act, 1)
                elif kind == "cum":
                    act.wait_ge(S["fe_in"], it["cum"] + 1)
                    nc.scalar.activation(fw[:, 2, :], fw[:, 1, :], ACT.Exp, scale=-1.0).then_inc(S["fe_out"], 1)
                    act.wait_ge(S["cum_full"], it["cum"] + 1)
                    act.wait_ge(S["line_stored"], 32)
                    act.wait_ge(S["zero_done"], 2 + l)
                    nc.scalar.activation(decay[0:NH, :].rearrange("p (c t) -> p c t", c=3), ps_s[0:NH, 0:3, 0:3 * BLK],
                                         ACT.Copy, scale=-1.0).then_inc(S["decay_hi"], 1)
                elif kind == "mt":
                    what = it["what"]
                    for (g, bank, _, nth), (c0, w) in zip(it["groups"], it["chunks"]):
                        act.wait_ge(S["pj_full"], g + 1)
                        ps = ps_s[:, bank, 0:w]
                        cs = slice(c0, c0 + w)
                        done = S["hi_done"]
                        if what == "IK":
                            for r in (0, HD):
                                a = nc.scalar.activation(parts[r:r + HD, 2, cs], ps[r:r + HD], ACT.Copy)
                        elif what in ("IQ", "Q"):
                            t = 4 * (it["p"] % 2) if what == "IQ" else 0
                            for e in range(2):
                                r = HD * e
                                a = nc.scalar.activation(parts[r:r + HD, t + e, cs], ps[r:r + HD], ACT.Copy, scale=A_SCALE)
                        elif what == "AQK":
                            h = it["h"]
                            nc.scalar.activation(qs[0:HD, h % 2, cs], ps[0:HD], ACT.Copy, scale=A_SCALE)
                            for r in (0, HD):
                                a = nc.scalar.activation(k_hi[r:r + HD, h % 2, cs], ps[HD:BLK], ACT.Copy)
                        elif what == "K":
                            for e in range(2):
                                for r in (0, HD):
                                    a = nc.scalar.activation(k_hi[r:r + HD, e, cs], ps[HD * e:HD * e + HD], ACT.Copy)
                        elif what == "G":
                            if it["upto"]["pv"]:
                                act.wait_ge(S["o_free"], it["upto"]["pv"])
                            a = nc.scalar.activation(gate[:, cs], ps, ACT.Tanh, scale=0.5)
                            done = S["gate_in"]
                        elif what == "KR":
                            continue
                        a.then_inc(done, 1)
                elif kind == "kb":
                    for (g, bank, _, nth), (c0, w) in zip(it["groups"], it["chunks"]):
                        act.wait_ge(S["pj_full"], g + 1)
                        nc.scalar.activation(k_t[0][0:HD, c0:c0 + w], ps_s[0:HD, bank, 0:w], ACT.Copy)
                        nc.scalar.activation(k_t[1][0:HD, c0:c0 + w], ps_s[HD:BLK, bank, 0:w],
                                             ACT.Copy).then_inc(S["pj_act"], 1)
                elif kind == "qb":
                    for (g, bank, _, nth), (c0, w) in zip(it["groups"], it["chunks"]):
                        act.wait_ge(S["pj_full"], g + 1)
                        nc.scalar.activation(q_t[it["h"] % 2][0:HD, c0:c0 + w], ps_s[0:HD, bank, 0:w], ACT.Copy,
                                             scale=B_SCALE).then_inc(S["half_done"], 1)
                elif kind == "ix":
                    act.wait_ge(S["relu_full"], it["ix"] + 1)
                    waits(act, it["rwaits"])
                    dst = probs[:, it["row"], PAD:PAD + it["n"]].rearrange("p (c t) -> p c t", c=it["nb"])
                    nc.scalar.activation(dst, ps_s[:, it["bank"]:it["bank"] + it["nb"], 0:it["w"]],
                                         ACT.Relu).then_inc(S["relu_done"], 1)
                elif kind == "qk":
                    br, i, step = it["br"], it["i"], it["step"]
                    M = ln_rows(i)
                    act.wait_ge(S["max_done"], step + 1)
                    waits(act, it["rwaits"])
                    if br == "D":
                        s0 = NH * l + it["h"]
                        nc.scalar.activation(esink[0:M, step % 4:step % 4 + 1], sink[0:M, s0:s0 + 1], ACT.Exp,
                                             bias=nmax[0:M, step % 4:step % 4 + 1]).then_inc(S["es_done"], 1)
                    off = p_off(br, i)
                    dst = probs[0:M, it["row"], off:off + it["n"]].rearrange("p (c t) -> p c t", c=it["nb"])
                    nc.scalar.activation(dst, ps_s[0:M, it["bank"]:it["bank"] + it["nb"], 0:it["w"]], ACT.Exp,
                                         bias=nmax[0:M, step % 4:step % 4 + 1],
                                         accum_out=psums[0:M, step % 4:step % 4 + 1]).then_inc(S["exp_done"], 1)
                elif kind == "tp":
                    i, og = it["i"], it["og"]
                    M = ln_rows(i)
                    c0 = BLK if (i and i % 2 == 0) else 0
                    if og >= 2:
                        act.wait_ge(S["pv_done"], og - 1)
                    act.wait_ge(S["ms_done"], it["upto"]["ms"])
                    for j in range(it["ntg"]):
                        tg = it["tg"] + j
                        if not by_act[tg]:
                            continue
                        act.wait_ge(S["t_full"], tg + 1)
                        for c, slot, k in runs([s for _, s in it["slots"][4 * j:4 * j + 4]]):
                            src = ps_t[:, tg % 2, c * BLK:(c + k) * BLK].rearrange("p (k t) -> p k t", k=k)[:, :, 0:M]
                            a = nc.scalar.activation(probs_t[:, og % 2, slot:slot + k, c0:c0 + M], src, ACT.Copy)
                        a.then_inc(t_act, 1)

        @block.vector
        def _(dve):
            chain = [0]

            def link(ins):
                chain[0] += 1
                ins.then_inc(S["dve_chain"], 1)
                dve.wait_ge(S["dve_chain"], chain[0])

            dve.wait_ge(S["consts"], 16 * 10)
            dve.tensor_copy(ident_b[:], ident[:])
            dve.tensor_copy(anti[:], anti_in)
            link(dve.tensor_tensor(f_tmp, upper1[:, 0:BLK], ident[:], ALU.subtract))
            dve.tensor_scalar(tri_b[:], f_tmp, NEG, None, ALU.mult)
            dve.tensor_scalar(nsink, sink, -1.0, None, ALU.mult).then_inc(S["small_done"], 1)
            dve.wait_ge(S["line_full"], 1)
            dve.tensor_tensor(line_sb, ps_o[0:NH, :, 0:LINE], lmask, ALU.add).then_inc(S["line_ready"], 1)

            top = {"next": TOP_OPS}

            def top_ops(l, count):
                for _ in range(count):
                    if top["next"] >= TOP_OPS:
                        return
                    i, r = NB - 1 - top["next"] // (TOPK // 4), top["next"] % (TOPK // 4)
                    top["next"] += 1
                    n = keys_of(i)
                    sc = score[:, s_off[i]:s_off[i] + n]
                    if r:
                        dve.wait_ge(S["top_step"], top["steps"])
                    if r % 2 == 0:
                        dve.max(top8, sc).then_inc(S["top_step"], 1)
                    else:
                        dve.match_replace(sc, top8, sc, TAKEN).then_inc(S["top_step"], 1)
                    top["steps"] = top.get("steps", 0) + 1
                    if r == TOPK // 4 - 1:
                        dve.wait_ge(S["top_step"], top["steps"])
                        m = sel[:, s_off[i]:s_off[i] + n]
                        if l > 0 and i == NB - 1:
                            dve.wait_ge(S["s_full"], c_end[l - 1])
                        link(dve.tensor_scalar(m, sc, TAKEN, NEG, ALU.is_gt, ALU.mult))
                        dve.tensor_tensor(m[:, n - BLK:n], m[:, n - BLK:n], tri_b[:], ALU.min
                                          ).then_inc(S["mask_done"], 1)

            for it in items:
                kind, l = it["kind"], it["l"]
                if kind == "ln":
                    ln, b = it["ln"], it["b"]
                    M, r = ln_rows(b), ln % 2
                    if b == 0 or (l == DEPTH - 1 and b == 1):
                        dve.wait_ge(S["lnp_ld"], 32 * (l + 2))
                        if l >= 0:
                            dve.wait_ge(S["pj_full"], vw_used[(l, "U")])
                    dve.wait_ge(r_ld[r], 16 * (ln // 2 + 1))
                    z = res_in[0:M, r, :]
                    if l >= 0:
                        dve.wait_ge(S["y_full"], it["upto"]["yy"])
                        bank = 2 * ((it["upto"]["yy"] - 1) % 2)
                        z = z_sum[0:M, r, :]
                        dve.scalar_tensor_tensor(z, res_in[0:M, r, :], ALPHA,
                                                 ps_s[0:M, bank:bank + 2, :].rearrange("p a b -> p (a b)"),
                                                 ALU.mult, ALU.add).then_inc(S["y_free"], 1)
                        dve.wait_ge(S["y_free"], it["upto"]["yy"])
                    for j in range(2):
                        st = dve.bn_stats(stats[0:M, r, 6 * j:6 * j + 6], z[:, 512 * j:512 * (j + 1)])
                    link(st)
                    dve.bn_aggr(mv[0:M, r, :], stats[0:M, r, :]).then_inc(S["ln_var"], 1)
                    dve.wait_ge(S["ln_rs"], ln + 1)
                    if ln >= 2:
                        dve.wait_ge(x_st[r], 16 * (ln // 2))
                        if it["xprev"]:
                            dve.wait_ge(S["t_full"], it["xprev"])
                    xn = x_new[0:M, r, :]
                    link(dve.tensor_scalar(xn, z, mv[0:M, r, 0:1], rstd[0:M, r, 0:1], ALU.subtract, ALU.mult))
                    link(dve.tensor_tensor(xn, xn, ln_g[0:M, :], ALU.mult))
                    dve.tensor_tensor(xn, xn, ln_b[0:M, :], ALU.add).then_inc(S["ln_done"], 1)
                elif kind == "cum":
                    dve.wait_ge(S["pj_act"], it["upto"]["pj_act"])
                    dve.tensor_scalar(iws, fz[:, :, NH:2 * NH], IW_SCALE, None, ALU.mult)
                    link(dve.tensor_tensor(f3[0], fz[:, :, 0:NH], bf[:, 72 * l:72 * (l + 1)]
                                           .rearrange("p (b h) -> p b h", b=NB), ALU.add))
                    link(dve.tensor_scalar(fw[:, 1, :], fw[:, 0, :], -1.0, None, ALU.mult))
                    dve.tensor_tensor(fw[:, 1, :], fw[:, 0, :], fw[:, 1, :], ALU.max).then_inc(S["fe_in"], 1)
                    dve.wait_ge(S["fe_out"], it["cum"] + 1)
                    e, s_, s2, acc = fw[:, 2, :], fw[:, 3, :], fw[:, 4, :], fw[:, 1, :]
                    link(dve.tensor_scalar(s_, e, 2.0, None, ALU.add))
                    link(dve.reciprocal(s_, s_))
                    link(dve.tensor_tensor(s_, s_, e, ALU.mult))
                    link(dve.tensor_tensor(s2, s_, s_, ALU.mult))
                    link(dve.tensor_scalar(acc, s2, 1.0 / 17, None, ALU.mult))
                    for d in (15, 13, 11, 9, 7, 5, 3):
                        link(dve.scalar_tensor_tensor(acc, acc, 1.0 / d, s2, ALU.add, ALU.mult))
                    link(dve.scalar_tensor_tensor(acc, acc, 1.0, s_, ALU.add, ALU.mult))
                    link(dve.tensor_scalar(fw[:, 0, :], fw[:, 0, :], 0.0, None, ALU.min))
                    link(dve.scalar_tensor_tensor(fw[:, 5, :], acc, -2.0, fw[:, 0, :], ALU.mult, ALU.add))
                    dve.tensor_scalar(f3[5][:, 0, :], f3[5][:, 0, :], rowmask, None, ALU.mult).then_inc(S["cum_in"], 1)
                    dve.wait_ge(S["decay_hi"], it["cum"] + 1)
                    dve.scalar_tensor_tensor(decay[32:32 + NH, :].rearrange("p (c t) -> p c t", c=3),
                                             ps_s[0:NH, 0:3, 0:3 * BLK], -1.0,
                                             decay[0:NH, :].bitcast(F32).rearrange("p (c t) -> p c t", c=3),
                                             ALU.mult, ALU.subtract).then_inc(S["cum_free"], 1)
                elif kind == "ix":
                    i, n, ix = it["i"], it["n"], it["ix"]
                    sc = score[:, s_off[i]:s_off[i] + n]
                    w = iws[:, i, 2 * it["p"] + it["e"]:2 * it["p"] + it["e"] + 1]
                    src = probs[:, it["row"], PAD:PAD + n]
                    dve.wait_ge(S["relu_done"], ix + 1)
                    if it["first"]:
                        if i == 2:
                            for j in range(2):
                                dve.wait_ge(x_st[j], 16 * len([m for m in range(it["upto"]["ln"]) if m % 2 == j]))
                            dve.wait_ge(S["t_full"], it["upto"]["tg"])
                        dve.tensor_scalar(sc, src, w, None, ALU.mult).then_inc(S["acc_done"], 1)
                    else:
                        dve.wait_ge(S["acc_done"], ix - 6)
                        dve.scalar_tensor_tensor(sc, src, w, sc, ALU.mult, ALU.add).then_inc(S["acc_done"], 1)
                    if it["last"]:
                        dve.wait_ge(S["acc_done"], ix + 1)
                        link(dve.tensor_tensor(sc[:, n - BLK:n], sc[:, n - BLK:n], tri_b[:], ALU.add))
                        if i == NB - 1:
                            top["next"] = 0
                elif kind == "mt":
                    what = it["what"]
                    if what == "G":
                        for (g, bank, _, nth), (c0, w) in zip(it["groups"], it["chunks"]):
                            gcount[0] += 1
                            dve.wait_ge(S["gate_in"], gcount[0])
                            dve.scalar_tensor_tensor(gate[:, c0:c0 + w], gate[:, c0:c0 + w], 1.0,
                                                     ps_s[:, bank, 0:w], ALU.add, ALU.mult).then_inc(S["pj_dve"], 1)
                    if what not in ("G", "KR"):
                        for j, ((g, bank, _, nth), (c0, w)) in enumerate(zip(it["groups"], it["chunks"])):
                            ps, cs = ps_s[:, bank, 0:w], slice(c0, c0 + w)
                            dve.wait_ge(S["hi_done"], it["hi"] + j + 1)
                            if what in ("IQ", "Q"):
                                t = 4 * (it["p"] % 2) if what == "IQ" else 0
                                work = [(HD * e, parts[:, t + e, cs], HD - HD * e, parts[:, t + e, cs], A_SCALE) for e in range(2)]
                            elif what == "IK":
                                work = [(r, parts[:, 2, cs], r, parts[:, 3, cs], 1.0) for r in (0, HD)]
                            elif what == "AQK":
                                e = it["h"] % 2
                                work = [(0, qs[:, e, cs], HD, qs[:, e, cs], A_SCALE)]
                                work += [(HD, k_hi[:, e, cs], r, k_lo[:, e, cs], 1.0) for r in (0, HD)]
                            else:
                                work = [(HD * e, k_hi[:, e, cs], r, k_lo[:, e, cs], 1.0) for e in range(2) for r in (0, HD)]
                            for r, hi, r2, lo, scale in work:
                                a = dve.scalar_tensor_tensor(lo[r2:r2 + HD], ps[r:r + HD], scale,
                                                             hi[r:r + HD].bitcast(F32), ALU.mult, ALU.subtract)
                            a.then_inc(S["pj_dve"], 1)
                    if what == "KR":
                        for (g, bank, _, nth), (c0, w) in zip(it["groups"], it["chunks"]):
                            dve.wait_ge(S["pj_full"], g + 1)
                            cs = slice(c0, c0 + w)
                            dve.tensor_tensor(rtmp[64:96, 0:w], ps_s[96:128, bank, 0:w], rope_t[96:128, cs], ALU.mult)
                            link(dve.tensor_tensor(k_t[0][64:96, cs], ps_s[64:96, bank, 0:w], rope_t[64:96, cs], ALU.mult))
                            link(dve.tensor_tensor(k_t[0][64:96, cs], k_t[0][64:96, cs], rtmp[64:96, 0:w], ALU.add))
                            dve.tensor_copy(k_t[1][64:96, cs], k_t[0][64:96, cs]).then_inc(S["pj_dve"], 1)
                    if what == "G":
                        top_ops(l, 2)
                elif kind == "qb":
                    for (g, bank, _, nth), (c0, w) in zip(it["groups"], it["chunks"]):
                        hcount[0] += 1
                        dve.wait_ge(S["half_done"], hcount[0])
                        q = q_t[it["h"] % 2][64:96, c0:c0 + w]
                        dve.scalar_tensor_tensor(rtmp[64:96, 0:w], ps_s[96:128, bank, 0:w], B_SCALE,
                                                 rope_t[96:128, c0:c0 + w], ALU.mult, ALU.mult)
                        link(dve.scalar_tensor_tensor(q, ps_s[64:96, bank, 0:w], B_SCALE,
                                                      rope_t[64:96, c0:c0 + w], ALU.mult, ALU.mult))
                        dve.tensor_tensor(q, q, rtmp[64:96, 0:w], ALU.add).then_inc(S["pj_dve"], 1)
                        dve.wait_ge(S["pj_dve"], nth)
                elif kind == "xt":
                    b = it["b"]
                    M = ln_rows(b)
                    for tg in (it["tg"], it["tg"] + 1):
                        if not by_act[tg]:
                            dve.wait_ge(S["t_full"], tg + 1)
                            src = ps_t[:, tg % 2, :].rearrange("p (c t) -> p c t", c=4)[:, :, 0:M]
                            k = 4 * (tg - it["tg"])
                            dve.tensor_copy(xT[:, k:k + 4, col0(b):col0(b) + M], src).then_inc(t_dve, 1)
                elif kind == "tp":
                    i, og = it["i"], it["og"]
                    M = ln_rows(i)
                    c0 = BLK if (i and i % 2 == 0) else 0
                    groups = [j for j in range(it["ntg"]) if not by_act[it["tg"] + j]]
                    if groups:
                        if og >= 2:
                            dve.wait_ge(S["pv_done"], og - 1)
                        dve.wait_ge(S["ms_done"], it["upto"]["ms"])
                    for j in groups:
                        tg = it["tg"] + j
                        dve.wait_ge(S["t_full"], tg + 1)
                        for c, slot, k in runs([s for _, s in it["slots"][4 * j:4 * j + 4]]):
                            src = ps_t[:, tg % 2, c * BLK:(c + k) * BLK].rearrange("p (k t) -> p k t", k=k)[:, :, 0:M]
                            t = dve.tensor_copy(probs_t[:, og % 2, slot:slot + k, c0:c0 + M], src)
                        t.then_inc(t_dve, 1)
                elif kind == "ct":
                    c = it["cn"]
                    tg, b = it["tg"], it["b"]
                    dve.wait_ge(S["cn_rs"], c + 1)
                    dve.tensor_scalar(cn[:, c % 2, 0:Q_RANK], cn[:, c % 2, 0:Q_RANK], crs[:, c % 2, 0:1], None, ALU.mult)
                    dve.tensor_scalar(cn[:, c % 2, Q_RANK:384], cn[:, c % 2, Q_RANK:384], crs[:, c % 2, 1:2], None,
                                      ALU.mult).then_inc(S["cn_done"], 1)
                    if not by_act[tg]:
                        dve.wait_ge(S["t_full"], tg + 1)
                        for j in range(3):
                            gain = gq[:, 2 * l + j:2 * l + j + 1] if j < 2 else gkv[:, l:l + 1]
                            t = dve.tensor_scalar(cT[:, j, b * BLK:(b + 1) * BLK], ps_t[:, tg % 2, j * BLK:(j + 1) * BLK],
                                                  gain, None, ALU.mult)
                        t.then_inc(t_dve, 1)
                elif kind == "qk":
                    br, step = it["br"], it["step"]
                    M = ln_rows(it["i"])
                    if br == "C" and it["h"] == 0 and it["i"] == NB - 1:
                        top_ops(l, TOP_OPS)
                    dve.wait_ge(S["s_full"], step + 1)
                    nm = nmax[0:M, step % 4:step % 4 + 1]
                    m = dve.tensor_reduce(nm, ps_s[0:M, it["bank"]:it["bank"] + it["nb"], 0:it["w"]], AX.XY,
                                          ALU.max, negate=True)
                    if br == "D":
                        link(m)
                        s0 = NH * l + it["h"]
                        m = dve.tensor_tensor(nm, nm, nsink[0:M, s0:s0 + 1], ALU.min)
                    m.then_inc(S["max_done"], 1)
                    if br != "C":
                        top_ops(l, 2 if it["i"] <= 2 else 1)
                elif kind == "rec":
                    step = it["step"]
                    M = ln_rows(it["i"])
                    c = slice(step % 4, step % 4 + 1)
                    dve.wait_ge(S["exp_done"], step + 1)
                    if it["br"] == "D":
                        dve.wait_ge(S["es_done"], it["ds"] + 1)
                        link(dve.tensor_tensor(psums[0:M, c], psums[0:M, c], esink[0:M, c], ALU.add))
                    link(dve.reciprocal(rinv[0:M, c], psums[0:M, c]))
                    off = p_off(it["br"], it["i"])
                    p = probs[0:M, it["row"], off:off + it["n"]]
                    dve.tensor_scalar(p, p, rinv[0:M, c], None, ALU.mult).then_inc(S["nrm_done"], 1)
                    top_ops(l, 1)
                elif kind == "pv":
                    og, a = it["og"], it["a"]
                    r0 = HD * (it["h"] % 2)
                    c0, w = (0, N_META) if a == 0 else (N_META + 256 * (a - 1), 256)
                    dve.wait_ge(S["pv_done"], og + 1)
                    if og >= 2:
                        dve.wait_ge(mx_st[og % 2], 16 * (og // 2))
                    dve.wait_ge(S["pj_dve"], gate_ready[og])
                    dve.scalar_tensor_tensor(mixg[r0:r0 + HD, og % 2, 0:w], ps_o[r0:r0 + HD, og % 2, 0:w], 0.5,
                                             gate[r0:r0 + HD, c0:c0 + w], ALU.mult, ALU.mult).then_inc(S["o_free"], 1)

        @block.gpsimd
        def _(pool):
            chain = [0]

            def link(ins):
                chain[0] += 1
                ins.then_inc(S["pool_chain"], 1)
                pool.wait_ge(S["pool_chain"], chain[0])

            def split_bias(hu):
                if hu >= 2 * DEPTH * NH:
                    return
                pool.wait_ge(h_ld, 16 * (hu + 1))
                if hu >= 2:
                    pool.wait_ge(S["s_full"], head_end[hu - 2])
                link(nc.gpsimd.tensor_copy(bias[:, hu % 2, 0, :], hankel[:]))
                nc.gpsimd.tensor_tensor(bias[:, hu % 2, 1, :], hankel[:], bias[:, hu % 2, 0, :].bitcast(F32),
                                        ALU.subtract).then_inc(S["bias_done"], 1)
                pool.wait_ge(S["bias_done"], hu + 1)

            nc.gpsimd.memset(xT[:, :, 0:PAD], 0.0).then_inc(S["zero_done"], 1)
            pool.wait_ge(S["consts"], 16 * 10)
            pool.wait_ge(S["zero_done"], 1)
            for it in items:
                kind, l = it["kind"], it["l"]
                if kind == "ln":
                    M, r = ln_rows(it["b"]), it["ln"] % 2
                    pool.wait_ge(S["ln_var"], it["ln"] + 1)
                    link(nc.gpsimd.tensor_scalar(rstd[0:M, r, 1:2], mv[0:M, r, 1:2], LN_EPS, None, ALU.add))
                    nc.gpsimd.tensor_tensor(rstd[0:M, r, 0:1], rstd[0:M, r, 1:2], halfneg[0:M, :],
                                            ALU.pow).then_inc(S["ln_rs"], 1)
                    pool.wait_ge(S["ln_rs"], it["ln"] + 1)
                elif kind == "tm" and it["what"] == "TB":
                    r = it["cn"] % 2
                    pool.wait_ge(S["pj_act"], it["groups"][0][3])
                    if it["cn"] >= 2:
                        pool.wait_ge(S["cn_done"], it["cn"] - 1)
                    link(nc.gpsimd.tensor_scalar(crs[:, r, 0:1], cstat[:, r, 0:1], 1.0 / Q_RANK, RMS_EPS,
                                                 ALU.mult, ALU.add))
                    link(nc.gpsimd.tensor_scalar(crs[:, r, 1:2], cstat[:, r, 1:2], 1.0 / KV_RANK, RMS_EPS,
                                                 ALU.mult, ALU.add))
                    link(nc.gpsimd.tensor_tensor(crs[:, r, 0:1], crs[:, r, 0:1], halfneg, ALU.pow))
                    nc.gpsimd.tensor_tensor(crs[:, r, 1:2], crs[:, r, 1:2], halfneg, ALU.pow).then_inc(S["cn_rs"], 1)
                    pool.wait_ge(S["cn_rs"], it["cn"] + 1)
                elif kind == "cum":
                    pool.wait_ge(S["line_stored"], 32)
                    pool.wait_ge(S["line_ready"], 1)
                    if l > 0:
                        pool.wait_ge(S["pj_full"], vw_used[(l - 1, "U")])
                    nc.gpsimd.memset(decay.bitcast(F32), 0.0).then_inc(S["zero_done"], 1)
                    pool.wait_ge(S["zero_done"], 2 + l)
                    for h in range(NH):
                        link(nc.gpsimd.tensor_scalar(head_rows[:, h * BLK:(h + 1) * BLK], ident[:], 0.0,
                                                     head_row[:, h:h + 1], ALU.mult, ALU.add))
                    pool.wait_ge(S["cum_free"], it["cum"] + 1)
                    nc.gpsimd.memset(small[:, 200:201], 0.0).then_inc(S["decay_done"], 1)
                    pool.wait_ge(S["decay_done"], l + 1)
                elif kind == "ms":
                    what = it["what"]
                    if what == "A":
                        pool.wait_ge(S["relu_full"], it["upto"]["ix"])
                        pool.wait_ge(S["relu_done"], it["upto"]["ix"])
                        link(nc.gpsimd.memset(probs[:, :, 0:PAD], 0.0))
                        link(nc.gpsimd.memset(probs_t[:, :, 8, 0:BLK], 0.0))
                        nc.gpsimd.memset(probs_t[:, :, 9, BLK:2 * BLK], 0.0).then_inc(S["ms_done"], 1)
                    else:
                        pool.wait_ge(S["s_full"], it["upto"]["step"])
                        for t in (q_t[0], q_t[1], k_t[0]):
                            link(nc.gpsimd.memset(t[96:BLK, :], 0.0))
                        nc.gpsimd.memset(k_t[1][96:BLK, :], 0.0).then_inc(S["ms_done"], 1)
                    pool.wait_ge(S["ms_done"], it["ms"] + 1)
                    if it["ms"] == 0:
                        split_bias(0)
                elif kind == "qk" and it["hu"] is not None and it["i"] == NB - 1:
                    split_bias(it["hu"] + 1)


def p_off(br, i):
    return BLK * (i - 1) if br == "D" and i >= 2 else PAD


def runs(slots):
    out = []
    for c, s in enumerate(slots):
        if out and out[-1][1] + out[-1][2] == s:
            out[-1] = (out[-1][0], out[-1][1], out[-1][2] + 1)
        else:
            out.append((c, s, 1))
    return out


def feature_tiles():
    off, at = {}, 0
    for name, size in (("a_q", 512), ("a_k", 512), ("a_v", 512), ("a_f", 8), ("a_g", 512), ("b_cq", 256),
                       ("b_ckv", 128), ("b_kr", 32), ("b_g", 512), ("c_q", 512), ("c_k", 128), ("c_v", 128),
                       ("c_iq", 512), ("c_ik", 64), ("c_iw", 8), ("c_g", 512), ("d_q", 512), ("d_k", 128),
                       ("d_v", 128), ("d_g", 512)):
        off[name] = at
        at += size
    r = lambda name, a, n: list(range(off[name] + a, off[name] + a + n))
    kr = r("b_kr", 0, 32) + r("b_kr", 16, 16) + r("b_kr", 0, 16)
    tiles = []
    for it in Plan().items:
        if it["kind"] == "mt" and it["l"] == 0 and it["wt"] == len(tiles):
            w, p, h = it["what"], it.get("p"), it.get("h")
            br = it.get("br", "").lower()
            tiles.append({"IK": lambda: r("c_ik", 0, 64) * 2, "IQ": lambda: r("c_iq", 128 * p, 128),
                          "AQK": lambda: r("a_q", 64 * h, 64) + r("a_k", 64 * h, 64),
                          "G": lambda: r(br + "_g", 128 * p, 128), "K": lambda: r(br + "_k", 0, 128),
                          "Q": lambda: r(br + "_q", 128 * p, 128), "KR": lambda: kr * 2}[w]())
    rows = {"w_tc": r("c_v", 0, 128) + r("d_v", 0, 128) + r("a_f", 0, 8) + r("c_iw", 0, 8),
            "w_ta": r("a_v", 0, 512), "w_tb": r("b_cq", 0, 256) + r("b_ckv", 0, 128)}
    return tiles, rows


def kernel(**inputs):
    import numpy as np
    import concourse.bacc as bacc
    from concourse.bass_utils import run_bass_kernel_spmd

    a = {k: np.asarray(v) for k, v in inputs.items()}
    L = DEPTH

    def parts(w):
        return np.ascontiguousarray(w.reshape(L, -1, BLK, w.shape[-1]).transpose(0, 2, 1, 3)).reshape(L, BLK, -1)

    def spread(v):
        return np.ascontiguousarray(np.broadcast_to(v.reshape(1, -1), (BLK, v.size)))

    tiles, rows = feature_tiles()
    arrays = {"x": a["x"], "meta_tokens": a["meta_tokens"], "rel_bias": a["rel_bias"]}
    arrays["w_feat"] = np.stack([parts(a["w_in"][:, :, t]) for t in tiles], axis=1)
    for name, cols in rows.items():
        arrays[name] = parts(a["w_in"][:, :, cols])
    hq = [96 * h + c for h in range(NH) for c in list(range(96)) + list(range(80, 96)) + list(range(64, 80))]
    arrays["u_q"] = parts(a["w_uq"][:, :, hq])
    arrays["u_k"] = parts(a["w_ukv"][:, :, [128 * h + c for h in range(NH) for c in range(64)]])
    arrays["u_v"] = parts(a["w_ukv"][:, :, [128 * h + 64 + c for h in range(NH) for c in range(64)]])
    arrays["w_out"] = parts(a["w_out"]).reshape(L, BLK, 16, D_MODEL)
    arrays["ln_g"] = np.stack([spread(v) for v in (a["ln0_g"], *a["ln_g"])])
    arrays["ln_b"] = np.stack([spread(v) for v in (a["ln0_b"], *a["ln_b"])])
    arrays["b_f"] = spread(np.broadcast_to(a["b_f"][:, None, :], (L, NB, NH)))
    f32 = np.float32
    arrays["ident"] = np.eye(BLK, dtype=f32)
    arrays["anti"] = np.ascontiguousarray(np.eye(BLK, dtype=f32)[::-1])
    arrays["upper1"] = np.concatenate([np.triu(np.ones((BLK, BLK), f32)), np.ones((BLK, 3 * BLK), f32)], 1)
    small = np.zeros((BLK, 24), f32)
    small[PAD:, 0] = 1.0
    small[:, 1] = -0.5
    small[:, 2:6] = a["mla_gq"].reshape(2 * L, BLK).T
    small[:, 6:8] = a["mla_gkv"].T
    small[:, 8:24] = a["sinks"].reshape(1, -1)
    arrays["small"] = small
    arrays["head_row"] = np.tile(np.eye(32, NH, dtype=f32), (BLK // 32, 1)) * (np.arange(BLK) < 64)[:, None].astype(f32)
    half = ROPE // 2
    freqs = (f32(10000.0) ** (-np.arange(half, dtype=f32) / f32(half))).astype(f32)
    ang = freqs[:, None] * np.arange(NTOK, dtype=f32)[None, :]
    cos, sin = np.cos(ang).astype(f32), np.sin(ang).astype(f32)
    arrays["rope_t"] = np.concatenate([np.zeros((64, NTOK), f32), cos, cos, -sin, sin])
    dist = 255 - np.arange(LINE)
    n = np.maximum(dist, 0)
    large = 16 + (np.log(np.maximum(n, 1) / 16.0) / np.log(8.0) * 16 + 1e-9).astype(np.int64)
    bucket = np.where(n < 16, n, np.minimum(large, 31))
    hot = (np.arange(32)[:, None] == bucket[None, :]).astype(f32)
    near = hot.copy()
    near[31] -= 1.0
    near[:, dist < 0] = 0.0
    inside = (dist >= 0) & (dist < 128)
    arrays["onehot"] = np.concatenate([near, hot * inside], 1).astype(f32)
    arrays["lmask"] = np.ascontiguousarray(np.broadcast_to(
        np.concatenate([np.zeros(LINE), np.where(inside, 0.0, NEG)]).astype(f32), (NH, 2 * LINE)))

    nc = bacc.Bacc("TRN2", target_bir_lowering=False, num_devices=1)
    arrays = {"in_" + k: np.ascontiguousarray(v) for k, v in arrays.items()}
    t_in = {k[3:]: nc.dram_tensor(k, v.shape, mybir.dt.from_np(v.dtype), kind="ExternalInput").ap()
            for k, v in arrays.items()}
    out = nc.dram_tensor("out", (1, SEQ, D_MODEL), F32, kind="ExternalOutput").ap()
    build(nc, t_in, out)
    r = run_bass_kernel_spmd(nc, [arrays], core_ids=[0])
    return r.results[0]["out"]
```
